# Optimizing a Trainium2 kernel written in Bass

```python
import math
import jax, jax.numpy as jnp
from jax import lax
import numpy as np

D_MODEL = 1024
BATCH = 1
SEQ = 256
DEPTH = 2

N_HEADS = 16
HEAD_DIM = D_MODEL // N_HEADS
D_FF = 4 * D_MODEL
N_A_LAYERS = DEPTH // 2
N_B_LAYERS = DEPTH - N_A_LAYERS
MOBA_BLOCK = 256
MOBA_TOPK = 3
MOBA_Q_CHUNK = 16
FOX_Q_BLOCK = 128
RMS_EPS = 1e-6
NEG_INF = -1e30


def rms_norm(x, g):
    xf = x.astype(jnp.float32)
    y = xf * lax.rsqrt(jnp.mean(xf * xf, axis=-1, keepdims=True) + RMS_EPS)
    return (y * g.astype(jnp.float32)).astype(x.dtype)

def alibi_slopes(n):
    return jnp.asarray(2.0 ** (-8.0 * np.arange(1, n + 1) / n), dtype=jnp.float32)

def split_heads(t):
    b, s, _ = t.shape
    return t.reshape(b, s, N_HEADS, HEAD_DIM).transpose(0, 2, 1, 3)

def merge_heads(t):
    b, h, s, d = t.shape
    return t.transpose(0, 2, 1, 3).reshape(b, s, h * d)

def squared_relu_mlp(x, w_up, w_down):
    return jnp.square(jax.nn.relu(x @ w_up)) @ w_down

def moba_attention(q, k, v):
    b, h, s, d = q.shape
    nb = -(-s // MOBA_BLOCK)
    pad = ((0, 0), (0, 0), (0, nb * MOBA_BLOCK - s), (0, 0))
    kb = jnp.pad(k, pad).reshape(b, h, nb, MOBA_BLOCK, d)
    vb = jnp.pad(v, pad).reshape(b, h, nb, MOBA_BLOCK, d)
    scale = 1.0 / math.sqrt(d)
    slopes = alibi_slopes(h)[None, :, None, None]
    n_sel = min(MOBA_TOPK, nb - 1)
    own_blk = jnp.arange(s) // MOBA_BLOCK
    bi = jnp.arange(b)[:, None, None, None]
    hi = jnp.arange(h)[None, :, None, None]

    if n_sel > 0:
        k_mean = jnp.mean(kb.astype(jnp.float32), axis=3)
        gate = jnp.einsum('bhsd,bhnd->bhsn', q.astype(jnp.float32), k_mean)
        past = jnp.arange(nb)[None, :] < own_blk[:, None]
        gate = jnp.where(past, gate, NEG_INF)
        _, sel = lax.top_k(gate, n_sel)
        sel_valid = jnp.arange(n_sel)[None, :] < own_blk[:, None]

    n_chunks = s // MOBA_Q_CHUNK
    blk_offs = jnp.arange(MOBA_BLOCK)

    def chunk(ci):
        t0 = ci * MOBA_Q_CHUNK
        qc = lax.dynamic_slice_in_dim(q, t0, MOBA_Q_CHUNK, axis=2)
        tq = t0 + jnp.arange(MOBA_Q_CHUNK)
        blk = t0 // MOBA_BLOCK
        k_own = lax.dynamic_index_in_dim(kb, blk, axis=2, keepdims=False)
        v_own = lax.dynamic_index_in_dim(vb, blk, axis=2, keepdims=False)
        ks_own = blk * MOBA_BLOCK + blk_offs
        dist_own = (tq[:, None] - ks_own[None, :]).astype(jnp.float32)
        s_own = (jnp.einsum('bhcd,bhkd->bhck', qc, k_own).astype(jnp.float32) * scale
                 - slopes * dist_own)
        s_own = jnp.where(dist_own >= 0, s_own, NEG_INF)
        if n_sel > 0:
            sel_c = lax.dynamic_slice_in_dim(sel, t0, MOBA_Q_CHUNK, axis=2)
            valid_c = lax.dynamic_slice_in_dim(sel_valid, t0, MOBA_Q_CHUNK, axis=0)
            k_sel = kb[bi, hi, sel_c]
            v_sel = vb[bi, hi, sel_c]
            ks_sel = sel_c[..., None] * MOBA_BLOCK + blk_offs
            dist_sel = (tq[:, None, None] - ks_sel).astype(jnp.float32)
            s_sel = (jnp.einsum('bhcd,bhcnkd->bhcnk', qc, k_sel).astype(jnp.float32) * scale
                     - slopes[..., None] * dist_sel)
            s_sel = jnp.where(valid_c[:, :, None], s_sel, NEG_INF)
            scores = jnp.concatenate(
                [s_sel.reshape(b, h, MOBA_Q_CHUNK, n_sel * MOBA_BLOCK), s_own], axis=-1)
            p = jax.nn.softmax(scores, axis=-1)
            p_sel = p[..., :n_sel * MOBA_BLOCK].reshape(b, h, MOBA_Q_CHUNK, n_sel, MOBA_BLOCK).astype(v.dtype)
            p_own = p[..., n_sel * MOBA_BLOCK:].astype(v.dtype)
            return (jnp.einsum('bhcnk,bhcnkd->bhcd', p_sel, v_sel)
                    + jnp.einsum('bhck,bhkd->bhcd', p_own, v_own))
        p_own = jax.nn.softmax(s_own, axis=-1).astype(v.dtype)
        return jnp.einsum('bhck,bhkd->bhcd', p_own, v_own)

    outs = lax.map(chunk, jnp.arange(n_chunks))
    return outs.transpose(1, 2, 0, 3, 4).reshape(b, h, s, d)

def shared_kv(h, kv_norm, w_kv, w_f, b_f):
    hn = rms_norm(h, kv_norm)
    k, v = jnp.split(hn @ w_kv, 2, axis=-1)
    log_f = jax.nn.log_sigmoid((hn @ w_f + b_f).astype(jnp.float32))
    c = jnp.cumsum(log_f, axis=1).transpose(0, 2, 1)
    return split_heads(k), split_heads(v), c

def forgetting_attention(q, k, v, c):
    b, h, s, d = q.shape
    scale = 1.0 / math.sqrt(d)
    kpos = jnp.arange(s)

    def block(qi):
        t0 = qi * FOX_Q_BLOCK
        qb = lax.dynamic_slice_in_dim(q, t0, FOX_Q_BLOCK, axis=2)
        cq = lax.dynamic_slice_in_dim(c, t0, FOX_Q_BLOCK, axis=2)
        tq = t0 + jnp.arange(FOX_Q_BLOCK)
        sc = (jnp.einsum('bhqd,bhkd->bhqk', qb, k).astype(jnp.float32) * scale
              + cq[..., None] - c[:, :, None, :])
        sc = jnp.where(kpos[None, :] <= tq[:, None], sc, NEG_INF)
        p = jax.nn.softmax(sc, axis=-1).astype(v.dtype)
        return jnp.einsum('bhqk,bhkd->bhqd', p, v)

    outs = lax.map(block, jnp.arange(s // FOX_Q_BLOCK))
    return outs.transpose(1, 2, 0, 3, 4).reshape(b, h, s, d)

def first_inputs(seed: int = 0) -> dict:
    key = jax.random.key(seed)
    ks = jax.random.split(key, 14)
    D, F, H = D_MODEL, D_FF, N_HEADS
    nrm = lambda k, shape, fan_in, gain=1.0: (gain * fan_in ** -0.5) * jax.random.normal(k, shape, jnp.float32)
    return {
        "x": jax.random.normal(ks[0], (BATCH, SEQ, D), jnp.float32),
        "attn_norm": 1.0 + 0.02 * jax.random.normal(ks[1], (DEPTH, D), jnp.float32),
        "moba_w_qkv": nrm(ks[2], (N_A_LAYERS, D, 3 * D), D),
        "fox_w_q": nrm(ks[3], (N_B_LAYERS, D, D), D),
        "w_o": nrm(ks[4], (DEPTH, D, D), D, 0.5),
        "kv_norm": 1.0 + 0.02 * jax.random.normal(ks[5], (D,), jnp.float32),
        "w_kv": nrm(ks[6], (D, 2 * D), D),
        "w_f": nrm(ks[7], (D, H), D),
        "b_f": 3.0 + 0.5 * jax.random.normal(ks[8], (H,), jnp.float32),
        "mlp_norm": 1.0 + 0.02 * jax.random.normal(ks[9], (DEPTH, D), jnp.float32),
        "w_up": nrm(ks[10], (DEPTH, D, F), D),
        "w_down": nrm(ks[11], (DEPTH, F, D), F, 0.5),
        "final_norm": 1.0 + 0.02 * jax.random.normal(ks[12], (D,), jnp.float32),
    }

def first_block(x, attn_norm, moba_w_qkv, fox_w_q, w_o, kv_norm, w_kv, w_f, b_f,
              mlp_norm, w_up, w_down, final_norm):
    h = x
    k_sh = v_sh = c_sh = None
    for layer in range(DEPTH):
        if layer == N_A_LAYERS:
            k_sh, v_sh, c_sh = shared_kv(h, kv_norm, w_kv, w_f, b_f)
        hn = rms_norm(h, attn_norm[layer])
        if layer < N_A_LAYERS:
            q, k, v = jnp.split(hn @ moba_w_qkv[layer], 3, axis=-1)
            mix = moba_attention(split_heads(q), split_heads(k), split_heads(v))
        else:
            q = split_heads(hn @ fox_w_q[layer - N_A_LAYERS])
            mix = forgetting_attention(q, k_sh, v_sh, c_sh)
        h = h + merge_heads(mix) @ w_o[layer]
        h = h + squared_relu_mlp(rms_norm(h, mlp_norm[layer]), w_up[layer], w_down[layer])
    return rms_norm(h, final_norm)


DEPTH_2 = 1

EXPAND = 2
D_MIX = EXPAND * D_MODEL
D_SSD = D_MIX // 2
D_MLA = D_MIX - D_SSD
SSD_HEAD_DIM = 64
SSD_HEADS = D_SSD // SSD_HEAD_DIM
SSD_GROUPS = 2
SSD_HPG = SSD_HEADS // SSD_GROUPS
SSD_STATE = 128
CONV_WIDTH = 4
CHUNK = 128
MLA_HEADS = 8
QK_NOPE = 64
QK_ROPE = 32
QK_DIM = QK_NOPE + QK_ROPE
V_HEAD = D_MLA // MLA_HEADS
Q_LORA = 384
KV_LORA = 256
ROPE_THETA = 10000.0
Q_BLOCK = 128
D_FF_2 = 2816
N_MOD = 9
EPS = 1e-6
D_CONV = D_SSD + 2 * SSD_GROUPS * SSD_STATE
IN_WIDTHS = (D_SSD, D_SSD, SSD_GROUPS * SSD_STATE, SSD_GROUPS * SSD_STATE,
             SSD_HEADS, Q_LORA, KV_LORA, QK_ROPE)
D_IN_PROJ = sum(IN_WIDTHS)
IN_SPLITS = tuple(int(v) for v in np.cumsum(IN_WIDTHS)[:-1])


def rmsnorm(x, w):
    xf = x.astype(jnp.float32)
    y = xf * lax.rsqrt(jnp.mean(xf * xf, axis=-1, keepdims=True) + EPS)
    return (y * w.astype(jnp.float32)).astype(x.dtype)

def modulate(h, shift, scale):
    return h * (1.0 + scale[:, None, :]) + shift[:, None, :]

def swiglu(h, w_gate, w_up, w_down):
    return (jax.nn.silu(h @ w_gate) * (h @ w_up)) @ w_down

def apply_rope(u, cos, sin):
    u1, u2 = jnp.split(u, 2, axis=-1)
    return jnp.concatenate([u1 * cos - u2 * sin, u2 * cos + u1 * sin], axis=-1)

def causal_depthwise_conv(u, w, b):
    out = lax.conv_general_dilated(
        u, w[:, None, :].astype(u.dtype), window_strides=(1,),
        padding=[(CONV_WIDTH - 1, 0)],
        dimension_numbers=('NWC', 'WIO', 'NWC'),
        feature_group_count=u.shape[-1])
    return out + b.astype(u.dtype)

def ssd_chunked(xh, dt, A, Bm, Cm):
    b, S = xh.shape[0], xh.shape[1]
    nc = S // CHUNK
    dtype = xh.dtype
    xdt = (xh * dt[..., None].astype(dtype)).reshape(b, nc, CHUNK, SSD_GROUPS, SSD_HPG, SSD_HEAD_DIM)
    Bc = Bm.reshape(b, nc, CHUNK, SSD_GROUPS, SSD_STATE)
    Cc = Cm.reshape(b, nc, CHUNK, SSD_GROUPS, SSD_STATE)
    a_cum = jnp.cumsum((dt * A).reshape(b, nc, CHUNK, SSD_GROUPS, SSD_HPG), axis=2)
    seg = a_cum[:, :, :, None] - a_cum[:, :, None, :]
    causal = jnp.tril(jnp.ones((CHUNK, CHUNK), dtype=bool))[None, None, :, :, None, None]
    Lmat = jnp.exp(jnp.where(causal, seg, -jnp.inf)).astype(dtype)
    cb = jnp.einsum('bclgn,bcsgn->bclsg', Cc, Bc)
    y_diag = jnp.einsum('bclsg,bclsgr,bcsgrp->bclgrp', cb, Lmat, xdt)
    decay_states = jnp.exp(a_cum[:, :, -1:] - a_cum).astype(dtype)
    states = jnp.einsum('bclgn,bclgr,bclgrp->bcgrpn', Bc, decay_states, xdt)
    chunk_decay = jnp.exp(a_cum[:, :, -1]).astype(dtype)

    def step(h, inp):
        s_c, d_c = inp
        return d_c[..., None, None] * h + s_c, h

    h0 = jnp.zeros_like(states[:, 0])
    _, prev = lax.scan(step, h0, (jnp.moveaxis(states, 1, 0), jnp.moveaxis(chunk_decay, 1, 0)))
    prev = jnp.moveaxis(prev, 0, 1)
    y_off = jnp.einsum('bclgn,bcgrpn,bclgr->bclgrp', Cc, prev, jnp.exp(a_cum).astype(dtype))
    return (y_diag + y_off).reshape(b, S, SSD_GROUPS, SSD_HPG, SSD_HEAD_DIM)

def mla_causal_attention(q_nope, q_rope, k_nope, k_rope, v):
    b, S = q_nope.shape[0], q_nope.shape[1]
    nblk = S // Q_BLOCK
    scale = 1.0 / math.sqrt(QK_DIM)
    qn_b = q_nope.reshape(b, nblk, Q_BLOCK, MLA_HEADS, QK_NOPE).swapaxes(0, 1)
    qr_b = q_rope.reshape(b, nblk, Q_BLOCK, MLA_HEADS, QK_ROPE).swapaxes(0, 1)
    starts = jnp.arange(nblk, dtype=jnp.int32) * Q_BLOCK
    k_idx = jnp.arange(S, dtype=jnp.int32)

    def one_block(args):
        qn, qr, start = args
        s = (jnp.einsum('bqhd,bkhd->bhqk', qn, k_nope)
             + jnp.einsum('bqhr,bkr->bhqk', qr, k_rope)).astype(jnp.float32) * scale
        q_idx = start + jnp.arange(Q_BLOCK, dtype=jnp.int32)
        mask = k_idx[None, :] <= q_idx[:, None]
        s = jnp.where(mask[None, None], s, -jnp.inf)
        p = jax.nn.softmax(s, axis=-1).astype(v.dtype)
        return jnp.einsum('bhqk,bkhv->bqhv', p, v)

    out = lax.map(one_block, (qn_b, qr_b, starts))
    return out.swapaxes(0, 1).reshape(b, S, MLA_HEADS * V_HEAD)

def hybrid_mixer(h, positions, w_in, conv_w, conv_b, dt_bias, a_log, d_skip, ssd_norm_w,
                 q_norm_w, w_uq, kv_norm_w, w_ukv, mla_norm_w, w_out):
    b, S = h.shape[0], h.shape[1]
    proj = h @ w_in
    z, xs, Bm, Cm, dt_raw, cq, ckv, k_rope_raw = jnp.split(proj, IN_SPLITS, axis=-1)

    xBC = jax.nn.silu(causal_depthwise_conv(jnp.concatenate([xs, Bm, Cm], axis=-1), conv_w, conv_b))
    xs, Bm, Cm = jnp.split(xBC, [D_SSD, D_SSD + SSD_GROUPS * SSD_STATE], axis=-1)
    dt = jax.nn.softplus(dt_raw.astype(jnp.float32) + dt_bias.astype(jnp.float32))
    A = -jnp.exp(a_log.astype(jnp.float32))
    xh = xs.reshape(b, S, SSD_GROUPS, SSD_HPG, SSD_HEAD_DIM)
    y = ssd_chunked(xh, dt.reshape(b, S, SSD_GROUPS, SSD_HPG), A.reshape(SSD_GROUPS, SSD_HPG),
                    Bm.reshape(b, S, SSD_GROUPS, SSD_STATE), Cm.reshape(b, S, SSD_GROUPS, SSD_STATE))
    y = y + d_skip.reshape(SSD_GROUPS, SSD_HPG)[:, :, None].astype(y.dtype) * xh
    yg = (y.reshape(b, S, D_SSD) * jax.nn.silu(z)).reshape(b, S, SSD_GROUPS, D_SSD // SSD_GROUPS)
    y_ssd = rmsnorm(yg, ssd_norm_w.reshape(SSD_GROUPS, D_SSD // SSD_GROUPS)).reshape(b, S, D_SSD)

    q = (rmsnorm(cq, q_norm_w) @ w_uq).reshape(b, S, MLA_HEADS, QK_DIM)
    q_nope, q_rope = jnp.split(q, [QK_NOPE], axis=-1)
    kv = (rmsnorm(ckv, kv_norm_w) @ w_ukv).reshape(b, S, MLA_HEADS, QK_NOPE + V_HEAD)
    k_nope, v = jnp.split(kv, [QK_NOPE], axis=-1)
    inv_freq = ROPE_THETA ** (-jnp.arange(0, QK_ROPE, 2, dtype=jnp.float32) / QK_ROPE)
    ang = positions[..., None].astype(jnp.float32) * inv_freq
    cos, sin = jnp.cos(ang).astype(h.dtype), jnp.sin(ang).astype(h.dtype)
    q_rope = apply_rope(q_rope, cos[:, :, None], sin[:, :, None])
    k_rope = apply_rope(k_rope_raw, cos, sin)
    attn = mla_causal_attention(q_nope, q_rope, k_nope, k_rope, v)
    y_mla = rmsnorm(attn, mla_norm_w)

    return jnp.concatenate([y_ssd, y_mla], axis=-1) @ w_out

def second_inputs(seed: int = 0) -> dict:
    key = jax.random.key(seed)
    ks = iter(jax.random.split(key, 40))

    def dense(shape, fan_in):
        return jax.random.normal(next(ks), shape, jnp.float32) * fan_in ** -0.5

    def gain(shape):
        return 1.0 + 0.05 * jax.random.normal(next(ks), shape, jnp.float32)

    def small(shape, s=0.02):
        return s * jax.random.normal(next(ks), shape, jnp.float32)

    L = DEPTH_2
    x = jax.random.normal(next(ks), (BATCH, SEQ, D_MODEL), jnp.float32)
    c = jax.random.normal(next(ks), (BATCH, D_MODEL), jnp.float32)
    offsets = jax.random.randint(next(ks), (BATCH, 1), 0, 1024, dtype=jnp.int32)
    positions = offsets + jnp.arange(SEQ, dtype=jnp.int32)[None, :]
    dt0 = jnp.exp(jax.random.uniform(next(ks), (L, SSD_HEADS), jnp.float32,
                                     math.log(1e-3), math.log(1e-1)))
    dt_bias = dt0 + jnp.log(-jnp.expm1(-dt0))
    a_log = jnp.log(jax.random.uniform(next(ks), (L, SSD_HEADS), jnp.float32, 1.0, 16.0))
    return {
        "x": x,
        "c": c,
        "positions": positions,
        "w_ada": dense((L, D_MODEL, N_MOD * D_MODEL), D_MODEL),
        "b_ada": small((L, N_MOD * D_MODEL)),
        "norm_ffn1": gain((L, D_MODEL)),
        "ffn1_w_gate": dense((L, D_MODEL, D_FF_2), D_MODEL),
        "ffn1_w_up": dense((L, D_MODEL, D_FF_2), D_MODEL),
        "ffn1_w_down": dense((L, D_FF_2, D_MODEL), D_FF_2),
        "norm_mix": gain((L, D_MODEL)),
        "w_in": dense((L, D_MODEL, D_IN_PROJ), D_MODEL),
        "conv_w": dense((L, CONV_WIDTH, D_CONV), CONV_WIDTH),
        "conv_b": small((L, D_CONV)),
        "dt_bias": dt_bias,
        "a_log": a_log,
        "d_skip": gain((L, SSD_HEADS)),
        "ssd_norm_w": gain((L, D_SSD)),
        "q_norm_w": gain((L, Q_LORA)),
        "w_uq": dense((L, Q_LORA, MLA_HEADS * QK_DIM), Q_LORA),
        "kv_norm_w": gain((L, KV_LORA)),
        "w_ukv": dense((L, KV_LORA, MLA_HEADS * (QK_NOPE + V_HEAD)), KV_LORA),
        "mla_norm_w": gain((L, D_MLA)),
        "w_out": dense((L, D_MIX, D_MODEL), D_MIX),
        "norm_ffn2": gain((L, D_MODEL)),
        "ffn2_w_gate": dense((L, D_MODEL, D_FF_2), D_MODEL),
        "ffn2_w_up": dense((L, D_MODEL, D_FF_2), D_MODEL),
        "ffn2_w_down": dense((L, D_FF_2, D_MODEL), D_FF_2),
        "norm_final": gain((D_MODEL,)),
    }

def second_block(x, c, positions, w_ada, b_ada, norm_ffn1, ffn1_w_gate, ffn1_w_up, ffn1_w_down,
              norm_mix, w_in, conv_w, conv_b, dt_bias, a_log, d_skip, ssd_norm_w,
              q_norm_w, w_uq, kv_norm_w, w_ukv, mla_norm_w, w_out,
              norm_ffn2, ffn2_w_gate, ffn2_w_up, ffn2_w_down, norm_final):
    c_act = jax.nn.silu(c)
    for l in range(DEPTH_2):
        mod = c_act @ w_ada[l] + b_ada[l]
        (sh1, sc1, g1, sh2, sc2, g2, sh3, sc3, g3) = jnp.split(mod, N_MOD, axis=-1)
        h = modulate(rmsnorm(x, norm_ffn1[l]), sh1, sc1)
        x = x + 0.5 * g1[:, None, :] * swiglu(h, ffn1_w_gate[l], ffn1_w_up[l], ffn1_w_down[l])
        h = modulate(rmsnorm(x, norm_mix[l]), sh2, sc2)
        x = x + g2[:, None, :] * hybrid_mixer(
            h, positions, w_in[l], conv_w[l], conv_b[l], dt_bias[l], a_log[l], d_skip[l],
            ssd_norm_w[l], q_norm_w[l], w_uq[l], kv_norm_w[l], w_ukv[l], mla_norm_w[l], w_out[l])
        h = modulate(rmsnorm(x, norm_ffn2[l]), sh3, sc3)
        x = x + 0.5 * g3[:, None, :] * swiglu(h, ffn2_w_gate[l], ffn2_w_up[l], ffn2_w_down[l])
    return rmsnorm(x, norm_final)


def setup_inputs(seed=0):
    out = dict(first_inputs(seed))
    for name, value in second_inputs(seed + 1).items():
        if name != "x":
            out[name + "_2"] = value
    return out


def reference(
    x, attn_norm, moba_w_qkv, fox_w_q, w_o, kv_norm, w_kv, w_f, b_f, mlp_norm, w_up, w_down,
    final_norm, c_2, positions_2, w_ada_2, b_ada_2, norm_ffn1_2, ffn1_w_gate_2, ffn1_w_up_2,
    ffn1_w_down_2, norm_mix_2, w_in_2, conv_w_2, conv_b_2, dt_bias_2, a_log_2, d_skip_2,
    ssd_norm_w_2, q_norm_w_2, w_uq_2, kv_norm_w_2, w_ukv_2, mla_norm_w_2, w_out_2, norm_ffn2_2,
    ffn2_w_gate_2, ffn2_w_up_2, ffn2_w_down_2, norm_final_2,
):
    x = first_block(
        x, attn_norm, moba_w_qkv, fox_w_q, w_o, kv_norm, w_kv, w_f, b_f, mlp_norm, w_up, w_down,
        final_norm,
    )
    return second_block(
        x, c_2, positions_2, w_ada_2, b_ada_2, norm_ffn1_2, ffn1_w_gate_2, ffn1_w_up_2,
        ffn1_w_down_2, norm_mix_2, w_in_2, conv_w_2, conv_b_2, dt_bias_2, a_log_2, d_skip_2,
        ssd_norm_w_2, q_norm_w_2, w_uq_2, kv_norm_w_2, w_ukv_2, mla_norm_w_2, w_out_2,
        norm_ffn2_2, ffn2_w_gate_2, ffn2_w_up_2, ffn2_w_down_2, norm_final_2,
    )


_drawn_inputs = setup_inputs


def setup_inputs(seed=0):
    import zlib

    import numpy as np

    out = dict(_drawn_inputs(seed))
    spreads = {}
    factors = {'attn_norm': 8.0,
     'kv_norm': 8.0,
     'mlp_norm': 3.275,
     'final_norm': 2.708,
     'conv_b_2': 7.442,
     'd_skip_2': 7.442,
     'ssd_norm_w_2': 3.302,
     'q_norm_w_2': 8.0,
     'kv_norm_w_2': 3.142,
     'mla_norm_w_2': 3.257,
     'norm_ffn2_2': 3.438}
    for name, (base, spread) in spreads.items():
        noise = np.random.default_rng([zlib.crc32(name.encode()), seed]).standard_normal(out[name].shape)
        drawn = base * np.exp(spread * noise) if base else spread * noise
        out[name] = __import__('jax').numpy.asarray(drawn.astype(out[name].dtype))
    for name, factor in factors.items():
        out[name] = (out[name] * factor).astype(out[name].dtype)
    return out
```

```python
from contextlib import ExitStack

import numpy as np
import concourse.bass as bass
from concourse import mybir

ALU = mybir.AluOpType
ACT = mybir.ActivationFunctionType
AX_X = mybir.AxisListType.X
F32 = mybir.dt.float32
F32R = mybir.dt.float32r
I32 = mybir.dt.int32
U32 = mybir.dt.uint32

P = 128
S = 256
TT = S // P
D = 1024
CT = D // P
H = 16
DH = D // H
F1 = 4096
F2 = 2816
HM = 8
QK = 96
NOPE = 64
ROPE = 32
VH = 128
QL = 384
KVL = 256
NEG = -1e30
EPS = 1e-6
SEG = S + P

Z0, XBC0, TAIL0 = 0, D, 2560
TAILW = 16 + QL + KVL + ROPE
DT0, CQ0, CKV0, KR0 = 0, 16, 16 + QL, 16 + QL + KVL

UNIT = 2048
AW = UNIT // CT
RING = 3
U_QK = 0
U_V = U_QK + 2 * D // AW
U_WO0 = U_V + 4
U_MLP0 = U_WO0 + 4
N_MLP = 2 * F1 // AW
U_K = U_MLP0 + N_MLP
U_VS = U_K + D // AW
U_Q = U_VS + 4
U_WO1 = U_Q + D // AW
U_MLP1 = U_WO1 + 4
U_FFN1 = U_MLP1 + N_MLP
N_FFN = 3 * F2 // AW
U_TAIL = U_FFN1 + N_FFN
U_Z = U_TAIL + 4
U_UQ = U_Z + 4
U_UKV = U_UQ + 2
U_XBC = U_UKV + 2
U_OUT = U_XBC + 6
U_FFN2 = U_OUT + 8
U_END = U_FFN2 + N_FFN

CH1 = F1 // AW
CH2 = F2 // AW
CHUNK0 = {"mlp0": 0, "mlp1": CH1, "ffn1": 2 * CH1, "ffn2": 2 * CH1 + CH2}
MLP_BODY = 3
FFN_BODY = 2

STAGES = ["attn0", "o0", "mlp0", "kv", "q", "o1", "mlp1", "ffn1", "mix", "lat", "mla", "ssd", "ffn2"]
PAIRS = {s: 3 if s == "lat" else 4 for s in STAGES}
PAIR0 = {s: sum(PAIRS[r] for r in STAGES[:i]) for i, s in enumerate(STAGES)}
TR_STAGES = [s for s in STAGES if s not in ("q", "o0", "o1")]
TR0 = {s: sum(PAIRS[r] for r in TR_STAGES[:i]) for i, s in enumerate(TR_STAGES)}
TR0["q"] = TR0["kv"]
NORMS = ["attn0", "mlp0", "kv", "mlp1", "final", "ffn1", "mix", "ffn2", "out"]
TBANK = [4, 6, 5, 7]

ROWS_A = [("attn_norm", 16), ("mlp_norm", 16), ("kv_norm", 8), ("norm_ffn1_2", 8), ("norm_mix_2", 8),
          ("norm_ffn2_2", 8), ("ssd_norm_w_2", 8), ("mla_norm_w_2", 8), ("q_norm_w_2", 3), ("kv_norm_w_2", 2),
          ("c_2", 8), ("conv_b_2", 12)]
ROWS_B = [("b_ada_2", 72), ("conv_w_2", 48)]
COL_A = {n: sum(k for _, k in ROWS_A[:i]) for i, (n, _) in enumerate(ROWS_A)}
COL_B = {n: sum(k for _, k in ROWS_B[:i]) for i, (n, _) in enumerate(ROWS_B)}
NA = sum(k for _, k in ROWS_A)
NB = sum(k for _, k in ROWS_B)

ADA_TILES = 24


def build(nc, t_in, out):
    g = t_in
    with ExitStack() as ctx:
        def sb(name, shape, dt=F32):
            return ctx.enter_context(nc.sbuf_tensor(name, shape, dt))

        def sem(name):
            return ctx.enter_context(nc.semaphore(name))

        raw = sb("raw", [P, RING, UNIT])
        whi = sb("whi", [P, RING, UNIT], F32R)
        wlo = sb("wlo", [P, RING, UNIT], F32R)
        x = sb("x", [P, TT, D])
        xn = sb("xn", [P, TT, D])
        ah = sb("ah", [P, CT, S], F32R)
        al = sb("al", [P, CT, S], F32R)
        bh = sb("bh", [P, CT, S], F32R)
        bl = sb("bl", [P, CT, S], F32R)
        hh = sb("hh", [P, MLP_BODY, 2, S], F32R)
        hl = sb("hl", [P, MLP_BODY, 2, S], F32R)
        work = sb("work", [P, 6 * SEG])
        stage = sb("stage", [P, 11264])
        gB = sb("gB", [P, D])
        nB = sb("nB", [P, D])
        ident = sb("ident", [P, P])
        identr = sb("identr", [P, P], F32R)
        maskq = sb("maskq", [P, P], F32R)
        maskt = sb("maskt", [P, P], F32R)
        cum = sb("cum", [P, S])
        dist = sb("dist", [P, SEG])
        vA = sb("vA", [P, NA])
        vB = sb("vB", [P, NB])
        wf = sb("wf", [P, CT, H])
        wfh = sb("wfh", [P, CT, H], F32R)
        wfl = sb("wfl", [P, CT, H], F32R)
        hb = sb("hb", [P, 4, H])
        modT = sb("modT", [P, 3, 24])
        mgain = sb("mgain", [P, 3, CT])
        cact = sb("cact", [P, CT])
        sums = sb("sums", [P, 8])
        newt = sb("newt", [P, 5, 4])
        mx = sb("mx", [P, 2, 2])
        nmx = sb("nmx", [P, 2, 2])
        rs = sb("rs", [P, TT, H])
        rinv = sb("rinv", [P, TT, H])
        aexp = sb("aexp", [P, H])
        sm = sb("sm", [P, 8, TT * H])
        rowh = sb("rowh", [P, S], F32R)
        rowl = sb("rowl", [P, S], F32R)
        rowf = sb("rowf", [P, S])
        trig = sb("trig", [P, 4, 2 * TT * 16])
        posi = sb("posi", [P, TT], I32)
        ps = ctx.enter_context(nc.psum_tensor("ps", [P, 8, 512], F32))

        wflat = work[:]
        hr = wflat[:, 0:512]
        hs = wflat[:, 512:1024]
        tb = wflat[:, 0:2 * SEG].rearrange("p (b n) -> p b n", b=2)
        pb = wflat[:, 2 * SEG:4 * SEG].rearrange("p (b n) -> p b n", b=2)
        pt = wflat[:, 4 * SEG:6 * SEG].rearrange("p (b n) -> p b n", b=2)
        st = stage[:]
        qT = st[:, 0:2048].rearrange("p (c n) -> p c n", c=CT)
        kT = st[:, 2048:4096].rearrange("p (c n) -> p c n", c=CT)
        vt = st[:, 4096:6144].rearrange("p (t n) -> p t n", t=TT)
        aslot = st[:, 6144:8192].rearrange("p (b c n) -> p b c n", b=2, c=CT)
        aacc = st[:, 8192:11264].rearrange("p (j n) -> p j n", j=ADA_TILES)
        rows = aacc
        z = st[:, 0:2048].rearrange("p (t n) -> p t n", t=TT)
        xsT = st[:, 2048:4096].rearrange("p (c n) -> p c n", c=CT)
        xdt = st[:, 2048:4096].rearrange("p (t n) -> p t n", t=TT)
        tail = st[:, 4096:4096 + TT * TAILW].rearrange("p (t n) -> p t n", t=TT)
        xs = st[:, 4096:6144].rearrange("p (t n) -> p t n", t=TT)
        vm = st[:, 6144:8192].rearrange("p (t n) -> p t n", t=TT)
        qtok = st[:, 8192:9728].rearrange("p (t n) -> p t n", t=TT)
        ktok = st[:, 9728:11264].rearrange("p (t n) -> p t n", t=TT)
        qTm = st[:, 8192:10240].rearrange("p (h n) -> p h n", h=HM)
        kTm = [st[:, 10240:11264].rearrange("p (h n) -> p h n", h=4), gB[:].rearrange("p (h n) -> p h n", h=4)]
        cb = st[:, 8192:8192 + 2 * SEG].rearrange("p (g n) -> p g n", g=2)
        sq_scratch = st[:, 9216:11264].rearrange("p (t n) -> p t n", t=TT)
        diag = st[:, 9216:10240].rearrange("p (c n) -> p c n", c=CT)
        bc = nB[:].rearrange("p (c n) -> p c n", c=4)
        tmp2 = wflat[:, 1024:2048].rearrange("p (b n) -> p b n", b=2)
        rope = wflat[:, 1024:2048].rearrange("p (k n) -> p k n", k=4)
        nac = sm[:, 7, :].rearrange("p (t h) -> p t h", t=TT)

        def conv_buf(u):
            return wflat[:, 512 * (u % 2):512 * (u % 2) + 512].rearrange("p (q n) -> p q n", q=2)

        def conv_w(tap, c):
            j = COL_B["conv_w_2"] + 12 * tap + c
            return vB[:, j:j + 1]

        w_landed = [sem(f"w_landed{r}") for r in range(RING)]
        w_hi = sem("w_hi")
        w_lo = sem("w_lo")
        w_used = sem("w_used")
        x_landed = sem("x_landed")
        rows_landed = sem("rows_landed")
        small_landed = sem("small_landed")
        nb_landed = sem("nb_landed")
        const = sem("const")
        rows_T = sem("rows_T")
        vecs = sem("vecs")
        x_ready = sem("x_ready")
        sq_done = sem("sq_done")
        xn_done = sem("xn_done")
        tr_done = sem("tr_done")
        in_hi = sem("in_hi")
        in_ready = sem("in_ready")
        dstep = sem("dstep")
        astep = sem("astep")
        pstep = sem("pstep")
        qk_copied = sem("qk_copied")
        tok_copied = sem("tok_copied")
        scored = sem("scored")
        biased = sem("biased")
        p_normed = sem("p_normed")
        half_done = sem("half_done")
        r_ready = sem("r_ready")
        xn1_done = sem("xn1_done")
        f_ps = sem("f_ps")
        f_copied = sem("f_copied")
        maxed = sem("maxed")
        exped = sem("exped")
        p_tr = sem("p_tr")
        p_copied = sem("p_copied")
        pv_done = sem("pv_done")
        o_ready = sem("o_ready")
        gated = sem("gated")
        h_sq = sem("h_sq")
        h_hi = sem("h_hi")
        h_ready = sem("h_ready")
        cact_done = sem("cact_done")
        a_landed = [sem(f"a_landed{b}") for b in range(2)]
        a_sum = sem("a_sum")
        a_red = sem("a_red")
        mod_done = sem("mod_done")
        diag_done = sem("diag_done")
        gate_ps = sem("gate_ps")
        gate_done = sem("gate_done")
        f_done = sem("f_done")
        sp_in = sem("sp_in")
        sp_exp = sem("sp_exp")
        sp_one = sem("sp_one")
        sp_ln = sem("sp_ln")
        lf_done = sem("lf_done")
        crow_ps = sem("crow_ps")
        row_f = sem("row_f")
        crow_hi = sem("crow_hi")
        crow_done = sem("crow_done")
        wf_hi = sem("wf_hi")
        wf_done = sem("wf_done")
        tok_copied2 = sem("tok_copied2")
        mq_tok2 = sem("mq_tok2")
        mqk_T = sem("mqk_T")
        mqk_copied = sem("mqk_copied")
        mqk_copied2 = sem("mqk_copied2")
        xs_tok2 = sem("xs_tok2")
        qtok_done = sem("qtok_done")
        lat_done = sem("lat_done")
        ssd_in = sem("ssd_in")
        mla_done = sem("mla_done")
        xdt_done = sem("xdt_done")
        tail_act = sem("tail_act")
        tail_dve = sem("tail_dve")
        lat_sq = sem("lat_sq")
        z_done = sem("z_done")
        ang_done = sem("ang_done")
        trig_done = sem("trig_done")
        al_exp = sem("al_exp")
        mq_tok = sem("mq_tok")
        conv0 = sem("conv0")
        conv_acc = sem("conv_acc")
        conv_out = sem("conv_out")
        xs_T = sem("xs_T")
        xs_tok = sem("xs_tok")
        cb_ps = sem("cb_ps")
        cb_done = sem("cb_done")
        ac_ps = sem("ac_ps")
        ac_done = sem("ac_done")
        row_ps = sem("row_ps")
        dec_exp = sem("dec_exp")
        dec_m = sem("dec_m")
        y_done = sem("y_done")
        y_ready = sem("y_ready")
        ssd_sq = sem("ssd_sq")
        mla_sq = sem("mla_sq")
        out_ready = sem("out_ready")
        stored = sem("stored")

        def tiles(w):
            return w.rearrange("(c p) n -> p c n", p=P)

        qkv = tiles(g["moba_w_qkv"][0])
        foxq = tiles(g["fox_w_q"][0])
        wo = [tiles(g["w_o"][l]) for l in range(2)]
        wkv = tiles(g["w_kv"])
        up = [tiles(g["w_up"][l]) for l in range(2)]
        down = [tiles(g["w_down"][l]) for l in range(2)]
        ffn = [[tiles(g[f"ffn{k}_w_{m}_2"][0]) for m in ("gate", "up", "down")] for k in (1, 2)]
        win = tiles(g["w_in_2"][0])
        uq = tiles(g["w_uq_2"][0])
        ukv = tiles(g["w_ukv_2"][0])
        wout = tiles(g["w_out_2"][0])
        ada = tiles(g["w_ada_2"][0])

        def slot(n):
            return n % RING

        def w_view(buf, s, kn, n):
            return buf[:, s, 0:kn * n].rearrange("p (c n) -> p c n", c=kn)

        def bank(b, n=512):
            return ps[:, b, 0:n]

        def banks(b, n):
            return ps[:].rearrange("p b n -> p (b n)")[:, 512 * b:512 * b + n]

        QK_UNITS = [*range(U_QK, U_V), *range(U_K, U_VS), *range(U_Q, U_WO1)]
        TOK_END = [U_WO0, U_Q, U_Z, U_UQ]
        RES_END = [U_MLP0, U_K, U_MLP1, U_FFN1, U_TAIL, U_FFN2, U_END]

        def up_end(n0, i, j, per, body):
            first = n0 + (1 if per == 2 else 2)
            later = n0 + per * j + (0 if per == 2 else 1)
            return (first if j == 0 else later) if isinstance(i, int) else i * (per * body) + later

        def qk_bank(m):
            return 4 + m % 3 if m < 8 else m % 2

        def unit_size(n):
            if U_TAIL <= n < U_Z:
                return 2 * TAILW
            if U_UQ <= n < U_XBC:
                return 768 if n == U_UQ + 1 else 2 * 768
            return UNIT

        block = ctx.enter_context(nc.Block())

        @block.sync
        def _(sp):
            for t in range(TT):
                sp.dma_start(x[:, t], g["x"][0, t * P:(t + 1) * P, :]).then_inc(x_landed, 16)

            def load(n, s, src, land=None):
                kn, w = src.shape[1], src.shape[2]
                if not isinstance(n, int) or n >= RING:
                    sp.wait_ge(w_lo, n - RING + 1)
                sp.dma_start(w_view(raw, s, kn, w), src).then_inc(w_landed[s], 16)

            def a_units(n0, w, col0, count):
                for u in range(count):
                    load(n0 + u, slot(n0 + u), w[:, :, col0 + u * AW:col0 + (u + 1) * AW])

            def d_units(n0, w, k0, count, cols):
                for u in range(count):
                    load(n0 + u, slot(n0 + u), w[:, k0 + 2 * u:k0 + 2 * u + 2, cols])

            def mlp(n0, l):
                load(n0, slot(n0), up[l][:, :, 0:AW])
                for i in [0]:
                    for j in range(MLP_BODY):
                        mlp_step(n0, l, i, j)
                with sp.Fori(1, (CH1 - 1) // MLP_BODY) as i:
                    for j in range(MLP_BODY):
                        mlp_step(n0, l, i, j)
                load(n0 + N_MLP - 1, slot(n0 + N_MLP - 1), down[l][:, 2 * CH1 - 2:2 * CH1, :])

            def mlp_step(n0, l, i, j):
                n = n0 + 1 + 2 * j
                load(i * (2 * MLP_BODY) + n, slot(n), up[l][:, :, bass.ds(i * (MLP_BODY * AW) + (j + 1) * AW, AW)])
                load(i * (2 * MLP_BODY) + (n + 1), slot(n + 1), down[l][:, bass.ds(i * (2 * MLP_BODY) + 2 * j, 2), :])

            def swiglu(n0, k):
                gate_w, up_w, down_w = ffn[k]
                load(n0, slot(n0), gate_w[:, :, 0:AW])
                load(n0 + 1, slot(n0 + 1), up_w[:, :, 0:AW])
                for j in range(FFN_BODY):
                    ffn_step(n0, k, 0, j)
                with sp.Fori(1, (CH2 - 1) // FFN_BODY) as i:
                    for j in range(FFN_BODY):
                        ffn_step(n0, k, i, j)
                load(n0 + N_FFN - 1, slot(n0 + N_FFN - 1), down_w[:, 2 * CH2 - 2:2 * CH2, :])

            def ffn_step(n0, k, i, j):
                gate_w, up_w, down_w = ffn[k]
                n = n0 + 2 + 3 * j
                col = i * (FFN_BODY * AW) + (j + 1) * AW
                load(i * (3 * FFN_BODY) + (n), slot(n), gate_w[:, :, bass.ds(col, AW)])
                load(i * (3 * FFN_BODY) + (n + 1), slot(n + 1), up_w[:, :, bass.ds(col, AW)])
                load(i * (3 * FFN_BODY) + (n + 2), slot(n + 2), down_w[:, bass.ds(i * (2 * FFN_BODY) + 2 * j, 2), :])

            a_units(U_QK, qkv, 0, 3)
            a_units(U_QK + 3, qkv, 3 * AW, 5)
            d_units(U_V, qkv, 0, 4, slice(2 * D, 3 * D))
            d_units(U_WO0, wo[0], 0, 4, slice(0, D))
            mlp(U_MLP0, 0)
            a_units(U_K, wkv, 0, 4)
            d_units(U_VS, wkv, 0, 4, slice(D, 2 * D))
            a_units(U_Q, foxq, 0, 4)
            d_units(U_WO1, wo[1], 0, 4, slice(0, D))
            mlp(U_MLP1, 1)
            swiglu(U_FFN1, 0)
            d_units(U_TAIL, win, 0, 4, slice(TAIL0, TAIL0 + TAILW))
            d_units(U_Z, win, 0, 4, slice(Z0, Z0 + D))
            load(U_UQ, slot(U_UQ), uq[:, 0:2, :])
            load(U_UQ + 1, slot(U_UQ + 1), uq[:, 2:3, :])
            for half in range(2):
                load(U_UKV + half, slot(U_UKV + half), ukv[:, :, half * 768:(half + 1) * 768])
            a_units(U_XBC, win, XBC0, 6)
            d_units(U_OUT, wout, CT, 4, slice(0, D))
            d_units(U_OUT + 4, wout, 0, 4, slice(0, D))
            swiglu(U_FFN2, 1)
            sp.wait_ge(y_ready, 4)
            sp.dma_start(nB[:], bass.AP(g["norm_final_2"].tensor, 0, [[0, P], [1, D]])).then_inc(nb_landed, 16)
            for t in range(TT):
                sp.wait_ge(out_ready, t + 1)
                sp.dma_start(out[0, t * P:(t + 1) * P, :], x[:, t]).then_inc(stored, 16)
            sp.wait_ge(stored, 16 * TT)

        @block.gpsimd
        def _(pool):
            G = nc.gpsimd
            n = [0]

            def link(ins):
                n[0] += 1
                ins.then_inc(pstep, 1)
                pool.wait_ge(pstep, n[0])

            link(G.memset(ident[:], 0.0))
            link(G.memset(cum[:], 1.0))
            link(G.affine_select(out=ident[:], in_=ident[:], compare_op=ALU.not_equal, fill=1.0, base=0,
                                 pattern=[[-1, P]], channel_multiplier=1))
            link(G.affine_select(out=cum[:, 0:P], in_=cum[:, 0:P], compare_op=ALU.is_ge, fill=0.0, base=0,
                                 pattern=[[1, P]], channel_multiplier=-1))
            link(G.iota(dist[:, 0:P], pattern=[[1, P]], base=0, channel_multiplier=-1,
                        allow_small_or_imprecise_dtypes=True))
            link(G.iota(dist[:, P:SEG], pattern=[[1, S]], base=-P, channel_multiplier=-1,
                        allow_small_or_imprecise_dtypes=True))
            link(G.affine_select(out=dist[:, 0:P], in_=dist[:, 0:P], compare_op=ALU.is_ge, fill=NEG, base=0,
                                 pattern=[[-1, P]], channel_multiplier=1))
            link(G.affine_select(out=dist[:, P:SEG], in_=dist[:, P:SEG], compare_op=ALU.is_ge, fill=NEG, base=P,
                                 pattern=[[-1, S]], channel_multiplier=1))
            link(G.memset(work[:, 0:P], 0.0))
            link(G.affine_select(out=work[:, P:2 * P], in_=work[:, 0:P], compare_op=ALU.is_ge, fill=NEG, base=0,
                                 pattern=[[-1, P]], channel_multiplier=1))
            link(G.affine_select(out=work[:, 2 * P:3 * P], in_=work[:, 0:P], compare_op=ALU.is_ge, fill=NEG, base=0,
                                 pattern=[[1, P]], channel_multiplier=-1))
            G.memset(rowh[:].bitcast(F32), 0.0)
            G.memset(rowl[:].bitcast(F32), 0.0)
            G.tensor_copy(identr[:], ident[:])
            G.tensor_copy(maskq[:], work[:, P:2 * P])
            G.tensor_copy(maskt[:], work[:, 2 * P:3 * P]).then_inc(const, 1)

            pool.wait_ge(cact_done, 1)
            for k in range(3):
                if k:
                    pool.wait_ge(a_red, k)

                def fetch(j, b):
                    pool.dma_start(aslot[:, b], ada[:, :, bass.ds(k * 3 * D + j * P, P)]).then_inc(a_landed[b], 16)

                def tile(j, b, r):
                    pool.wait_ge(a_landed[b], 16 * (k * (ADA_TILES // 2) + 1) + r * 16)
                    base = 4 * (k * ADA_TILES + b)
                    v = aslot[:, b]
                    G.tensor_tensor(v, v, cact[:].unsqueeze(2).to_broadcast([P, CT, P]), ALU.mult).then_inc(a_sum, 1)
                    pool.wait_ge(a_sum, base + 1 + r * 8)
                    G.tensor_tensor(v[:, 0:4], v[:, 0:4], v[:, 4:8], ALU.add).then_inc(a_sum, 1)
                    pool.wait_ge(a_sum, base + 2 + r * 8)
                    G.tensor_tensor(v[:, 0:2], v[:, 0:2], v[:, 2:4], ALU.add).then_inc(a_sum, 1)
                    pool.wait_ge(a_sum, base + 3 + r * 8)
                    G.tensor_tensor(aacc[:, bass.ds(j, 1), :], v[:, 0:1], v[:, 1:2], ALU.add).then_inc(a_sum, 1)
                    pool.wait_ge(a_sum, base + 4 + r * 8)

                for b in range(2):
                    fetch(b, b)
                with pool.Fori(0, ADA_TILES // 2 - 1) as r:
                    for b in range(2):
                        tile(r * 2 + b, b, r)
                        fetch(r * 2 + (b + 2), b)
                for b in range(2):
                    tile(ADA_TILES - 2 + b, b, ADA_TILES // 2 - 1)

        @block.scalar
        def _(act):
            A = nc.scalar
            done = [0]

            def split(n, s, size=UNIT):
                act.wait_ge(w_landed[s], landed(n, s))
                if not isinstance(n, int) or n >= RING:
                    act.wait_ge(w_used, used(n))
                A.activation(whi[:, s, 0:size], raw[:, s, 0:size], ACT.Copy).then_inc(w_hi, 1)

            def landed(n, s):
                if isinstance(n, int):
                    return 16 * (n // RING + 1)
                b, i = n
                return i * 32 + 16 * (b // RING + 1)

            def used(n):
                if isinstance(n, int):
                    return n - RING + 1
                b, i = n
                return i * 6 + (b - RING + 1)

            def splits(upto):
                while done[0] <= upto:
                    split(done[0], slot(done[0]), unit_size(done[0]))
                    done[0] += 1

            def square(j):
                for t in range(TT):
                    if j == 0:
                        act.wait_ge(x_landed, 16 * TT)
                    else:
                        act.wait_ge(x_ready, 2 * (j - 1) + t + 1)
                    A.activation(xn[:, t], x[:, t], ACT.Square, accum_out=sums[:, t:t + 1]).then_inc(sq_done, 1)

            def gained(stage_name, dst, gain, shift=None, npairs=4, bank_of=TBANK, ntiles=CT):
                for j in range(npairs):
                    act.wait_ge(tr_done, TR0[stage_name] + j + 1)
                    if stage_name == "q":
                        act.wait_ge(in_ready, PAIR0["kv"] + j + 1)
                    n = min(2, ntiles - 2 * j)
                    for q in range(n):
                        c = 2 * j + q
                        src = ps[:, bank_of[j], q * S:(q + 1) * S]
                        if shift is None:
                            ins = A.activation(dst[:, c], src, ACT.Copy, scale=gain(c))
                        else:
                            ins = A.activation(dst[:, c], src, ACT.Identity, scale=gain(c), bias=shift(c))
                    ins.then_inc(in_hi, 1)

            def scale_rows(idx):
                act.wait_ge(r_ready, idx + 1)
                A.activation(xn[:, 1], x[:, 1], ACT.Copy, scale=newt[:, 2, 1:2]).then_inc(xn1_done, 1)

            def gate_copy(k, factor):
                act.wait_ge(gate_ps, k + 1)
                A.activation(gB[:, 0:512], bank(5), ACT.Copy, scale=factor)
                A.activation(gB[:, 512:D], bank(7), ACT.Copy, scale=factor).then_inc(gate_done, 1)

            def plain(h0, j, dst):
                act.wait_ge(pv_done, h0 + 4 * (j + 1))
                A.activation(dst[:, 2 * j:2 * j + 2].rearrange("p c n -> p (c n)"), bank(TBANK[j]),
                             ACT.Copy).then_inc(in_hi, 1)

            def qk_copy(m, dst, pair):
                act.wait_ge(w_used, QK_UNITS[m] + 1)
                A.activation(dst[:, 2 * pair:2 * pair + 2].rearrange("p c n -> p (c n)"), bank(qk_bank(m)),
                             ACT.Copy).then_inc(qk_copied, 1)

            def head_exp(hg, h, src, scale):
                act.wait_ge(maxed, hg + 1)
                if h >= 2:
                    act.wait_ge(p_tr, hg - 1)
                b = h % 2
                A.activation(pb[:, b, 0:P], src(b)[:, 0:P], ACT.Exp, bias=nmx[:, b, 0:1], scale=scale,
                             accum_out=rs[:, 0, h:h + 1])
                A.activation(pb[:, b, P:SEG], src(b)[:, P:SEG], ACT.Exp, bias=nmx[:, b, 1:2], scale=scale,
                             accum_out=rs[:, 1, h:h + 1]).then_inc(exped, 1)

            def p_copy(hg, h):
                act.wait_ge(p_tr, hg + 1)
                if h >= 2:
                    act.wait_ge(pv_done, hg - 1)
                A.activation(pt[:, h % 2], bank(2 + h % 2, SEG), ACT.Copy).then_inc(p_copied, 1)

            def heads(h0, count, src, scale):
                for h in range(count):
                    head_exp(h0 + h, h, src, scale)
                    if h:
                        p_copy(h0 + h - 1, h - 1)
                p_copy(h0 + count - 1, count - 1)

            def block_heads(h0, src):
                for h in range(H):
                    head_exp(h0 + h, h, src, DH ** -0.5)
                    if h:
                        p_copy(h0 + h - 1, h - 1)
                    if h >= 6 and h % 4 == 2:
                        plain(h0, h // 4 - 1, ah)
                p_copy(h0 + H - 1, H - 1)
                plain(h0, 3, ah)

            def tok_copy(idx, b0, dst):
                act.wait_ge(w_used, TOK_END[idx])
                A.activation(dst, banks(b0, dst.shape[1]), ACT.Copy).then_inc(tok_copied, 1)

            def chunk(cs, used_units, b, silu, buf):
                cs1 = cs + 1
                act.wait_ge(w_used, used_units)
                if not isinstance(cs, int) or cs > 0:
                    act.wait_ge(h_sq, cs)
                    act.wait_ge(h_hi, cs)
                if silu:
                    A.activation(hr, bank(b), ACT.Silu).then_inc(gated, 1)
                    act.wait_ge(h_sq, cs1)
                    A.activation(hh[:, buf].rearrange("p c n -> p (c n)"), hs, ACT.Copy).then_inc(h_hi, 1)
                else:
                    A.activation(hr, bank(b), ACT.Relu).then_inc(gated, 1)
                    act.wait_ge(gated, cs1)
                    A.activation(hh[:, buf].rearrange("p c n -> p (c n)"), hr, ACT.Square).then_inc(h_hi, 1)

            def mlp(n0, c0):
                def body(i):
                    for j in range(MLP_BODY):
                        chunk(i * MLP_BODY + (c0 + j), up_end(n0, i, j, 2, MLP_BODY), 4 + j, False, j)
                        for q in range(2):
                            n = n0 + 2 * j + 2 + q
                            split(n if isinstance(i, int) else (n, i), slot(n))
                body(0)
                with act.Fori(1, (CH1 - 1) // MLP_BODY) as i:
                    body(i)
                done[0] = n0 + N_MLP
                chunk(c0 + CH1 - 1, n0 + 2 * (CH1 - 1), 4, False, 0)

            def swiglu(n0, c0):
                def body(i):
                    for j in range(FFN_BODY):
                        n = n0 + 3 * j + 2
                        split(n if isinstance(i, int) else (n, i), slot(n))
                        chunk(i * FFN_BODY + (c0 + j), up_end(n0, i, j, 3, FFN_BODY), 4 + 2 * j, True, j)
                        for q in (1, 2):
                            split(n + q if isinstance(i, int) else (n + q, i), slot(n + q))
                body(0)
                with act.Fori(1, (CH2 - 1) // FFN_BODY) as i:
                    body(i)
                done[0] = n0 + N_FFN - 1
                splits(n0 + N_FFN - 1)
                chunk(c0 + CH2 - 1, n0 + 3 * (CH2 - 1) + 1, 4, True, 0)

            col = lambda tab, cols, name, off=0: (lambda c: tab[:, cols[name] + off + c:cols[name] + off + c + 1])

            for tbl, (names, row0) in enumerate(((ROWS_A, COL_A), (ROWS_B, COL_B))):
                for name, k in names:
                    v = g[name]
                    src = {1: lambda: v.rearrange("(r n) -> r n", n=P),
                           2: lambda: v.rearrange("l (r n) -> (l r) n", n=P),
                           3: lambda: v.rearrange("l j (r n) -> (l j r) n", n=P)}[len(v.shape)]()
                    act.dma_start(rows[row0[name]:row0[name] + k, tbl, :], src).then_inc(rows_landed, 16)
            for j, name in enumerate(("b_f", "dt_bias_2", "a_log_2", "d_skip_2")):
                act.dma_start(hb[:, j, :], bass.AP(g[name].tensor, 0, [[0, P], [1, H]])).then_inc(small_landed, 16)
            act.dma_start(wf[:], tiles(g["w_f"])).then_inc(small_landed, 16)
            for t in range(TT):
                act.dma_start(posi[:, t:t + 1],
                             g["positions_2"][0:1, t * P:(t + 1) * P].rearrange("a p -> p a")).then_inc(small_landed, 16)
            act.dma_start(nB[:], bass.AP(g["final_norm"].tensor, 0, [[0, P], [1, D]])).then_inc(nb_landed, 16)
            square(0)
            splits(2)
            act.wait_ge(vecs, 1)
            A.activation(cact[:], vA[:, COL_A["c_2"]:COL_A["c_2"] + CT], ACT.Silu).then_inc(cact_done, 1)
            scale_rows(0)
            gained("attn0", ah, col(vA, COL_A, "attn_norm"))
            act.wait_ge(small_landed, 16 * (5 + TT))
            A.activation(wfh[:], wf[:], ACT.Copy).then_inc(wf_hi, 1)
            for m in range(8):
                qk_copy(m, qT if m < 4 else kT, m % 4)
                splits(m + 3)
            splits(U_WO0 + 1)
            tok_copy(0, 0, vt[:, 0])
            splits(U_WO0 + 2)
            block_heads(0, lambda b: tb[:, b])
            splits(U_MLP0 + 1)
            square(1)
            scale_rows(1)
            gained("mlp0", ah, col(vA, COL_A, "mlp_norm"))
            mlp(U_MLP0, 0)
            splits(U_K + 1)
            square(2)
            scale_rows(2)
            gained("kv", ah, col(vA, COL_A, "kv_norm"))
            gained("q", bh, col(vA, COL_A, "attn_norm", CT))
            splits(U_K + 2)
            act.wait_ge(sp_in, 1)
            A.activation(sm[:, 2], sm[:, 1], ACT.Exp).then_inc(sp_exp, 1)
            act.wait_ge(sp_one, 1)
            A.activation(sm[:, 4], sm[:, 3], ACT.Ln).then_inc(sp_ln, 1)
            for m in range(4):
                qk_copy(8 + m, kT, m)
                splits(U_K + m + 3)
            act.wait_ge(row_f, 1)
            A.activation(rowh[0:H], rowf[0:H], ACT.Copy).then_inc(crow_hi, 1)
            splits(U_Q + 1)
            tok_copy(1, 4, vt[:, 0])
            for m in range(4):
                splits(U_Q + m + 2)
                qk_copy(12 + m, qT, m)
            splits(U_WO1 + 2)
            block_heads(H, lambda b: bank(b, SEG))
            splits(U_MLP1 + 1)
            square(3)
            scale_rows(3)
            gained("mlp1", ah, col(vA, COL_A, "mlp_norm", CT))
            mlp(U_MLP1, CHUNK0["mlp1"])
            splits(U_FFN1 + 1)
            square(4)
            gate_copy(0, 0.5)
            square(5)
            scale_rows(4)
            act.wait_ge(mod_done, 3)
            mod = lambda k: (lambda c: mgain[:, k, c:c + 1], lambda c: modT[:, k, c:c + 1])
            gained("ffn1", ah, *mod(0))
            swiglu(U_FFN1, CHUNK0["ffn1"])
            splits(U_TAIL + 1)
            square(6)
            scale_rows(5)
            gained("mix", ah, *mod(1))
            splits(U_TAIL + 5)

            act.wait_ge(w_used, TOK_END[2])
            A.activation(tail[:, 0], banks(0, TAILW), ACT.Copy).then_inc(tail_act, 1)
            act.wait_ge(tail_act, 1)
            act.wait_ge(tail_dve, 1)
            for t in range(TT):
                A.activation(xn[:, t, 0:QL], tail[:, t, CQ0:CQ0 + QL], ACT.Square, accum_out=sums[:, t:t + 1])
                ins = A.activation(xn[:, t, QL:QL + KVL], tail[:, t, CKV0:CKV0 + KVL], ACT.Square,
                                   accum_out=sums[:, 2 + t:3 + t])
            ins.then_inc(lat_sq, 1)
            act.wait_ge(sp_in, 2)
            A.activation(sm[:, 2], sm[:, 1], ACT.Exp).then_inc(sp_exp, 1)
            A.activation(aexp[:], hb[:, 2], ACT.Exp).then_inc(al_exp, 1)
            act.wait_ge(sp_one, 2)
            A.activation(sm[:, 4], sm[:, 3], ACT.Ln).then_inc(sp_ln, 1)
            act.wait_ge(ang_done, 1)
            A.activation(trig[:, 3], trig[:, 2], ACT.Sin).then_inc(trig_done, 1)
            splits(U_Z + 5)
            for t in range(TT):
                act.wait_ge(w_used, TOK_END[3])
                ins = A.activation(z[:, t], banks(4 + 2 * t, D), ACT.Silu)
            ins.then_inc(z_done, 1)
            gained("lat", bh, lambda c: (vA[:, COL_A["q_norm_w_2"] + c:COL_A["q_norm_w_2"] + c + 1]),
                   npairs=3, bank_of=[0, 1, 2], ntiles=5)
            splits(U_UKV + 1)
            act.wait_ge(w_used, U_UKV)
            A.activation(qtok[:, 0], banks(4, 768), ACT.Copy).then_inc(mq_tok, 1)
            for half in range(2):
                act.wait_ge(w_used, U_UKV + 1 + half)
                src = banks(4 * half, 768).rearrange("p (h n) -> p h n", h=4)
                A.activation(ktok[:, 0].rearrange("p (h n) -> p h n", h=HM)[:, 4 * half:4 * half + 4, 0:NOPE],
                             src[:, :, 0:NOPE], ACT.Copy)
                A.activation(vm[:, 0].rearrange("p (h n) -> p h n", h=HM)[:, 4 * half:4 * half + 4],
                             src[:, :, NOPE:192], ACT.Copy).then_inc(mq_tok, 1)
            splits(U_XBC + 1)
            for u in range(6):
                act.wait_ge(w_used, U_XBC + u + 1)
                if u >= 2:
                    act.wait_ge(conv_out, u - 1)
                for q in range(2):
                    c = 2 * u + q
                    ins = A.activation(conv_buf(u)[:, q], ps[:, u % 3, q * S:(q + 1) * S], ACT.Identity,
                                       scale=conv_w(3, c), bias=vA[:, COL_A["conv_b_2"] + c:COL_A["conv_b_2"] + c + 1])
                ins.then_inc(conv0, 1)
                splits(U_XBC + u + 2)
                act.wait_ge(conv_acc, u + 1)
                dst = xsT[:, 2 * u:2 * u + 2] if u < 4 else bc[:, 2 * (u - 4):2 * (u - 4) + 2]
                A.activation(dst, conv_buf(u), ACT.Silu).then_inc(conv_out, 1)
            splits(U_OUT + 2)
            act.wait_ge(xs_T, 1)
            A.activation(xs[:, 0], banks(4, D), ACT.Copy).then_inc(xs_tok, 1)
            act.wait_ge(mqk_T, 1)
            for b in range(4):
                ins = A.activation(qTm[0:QK, 2 * b:2 * b + 2], ps[0:QK, 4 + b].rearrange("p (h n) -> p h n", h=2), ACT.Copy)
            ins.then_inc(mqk_copied, 1)
            heads(2 * H, HM, lambda b: bank(b, SEG), QK ** -0.5)
            act.wait_ge(o_ready, 4)
            for t in range(TT):
                ins = A.activation(sq_scratch[:, t], xn[:, t], ACT.Square, accum_out=sums[:, t:t + 1])
            ins.then_inc(mla_sq, 1)
            gained("mla", bh, col(vA, COL_A, "mla_norm_w_2"))
            act.wait_ge(row_f, 2)
            A.activation(rowh[0:H], rowf[0:H], ACT.Copy).then_inc(crow_hi, 1)
            act.wait_ge(ac_done, 1)
            for h in range(H):
                act.wait_ge(row_ps, h + 1)
                if h >= 2:
                    act.wait_ge(dec_m, h - 1)
                b = h % 2
                A.activation(tb[:, b, 0:S], bank(b, S), ACT.Exp, bias=nac[:, 0, h:h + 1])
                A.activation(tb[:, b, S:SEG], ps[:, b, S:SEG], ACT.Exp, bias=nac[:, 1, h:h + 1]).then_inc(dec_exp, 1)
            for t in range(TT):
                act.wait_ge(y_ready, t + 1)
                for gr in range(2):
                    ins = A.activation(xn[:, t, 512 * gr:512 * gr + 512], xs[:, t, 512 * gr:512 * gr + 512],
                                       ACT.Square, accum_out=sums[:, 2 * t + gr:2 * t + gr + 1])
                ins.then_inc(ssd_sq, 1)
            splits(U_OUT + 3)
            gained("ssd", ah, col(vA, COL_A, "ssd_norm_w_2"))
            splits(U_FFN2 + 1)
            square(7)
            gate_copy(2, 0.5)
            scale_rows(6)
            gained("ffn2", ah, *mod(2))
            swiglu(U_FFN2, CHUNK0["ffn2"])
            square(8)

        @block.vector
        def _(dve):
            V = nc.vector
            n = [0]
            done = [0]

            def link(ins):
                n[0] += 1
                ins.then_inc(dstep, 1)
                dve.wait_ge(dstep, n[0])

            def split(u, s, size=UNIT):
                if isinstance(u, int):
                    dve.wait_ge(w_hi, u + 1)
                else:
                    dve.wait_ge(w_hi, u[1] * 6 + (u[0] + 1))
                V.tensor_tensor(wlo[:, s, 0:size], raw[:, s, 0:size], whi[:, s, 0:size].bitcast(F32),
                                ALU.subtract).then_inc(w_lo, 1)

            def splits(upto):
                while done[0] <= upto:
                    split(done[0], slot(done[0]), unit_size(done[0]))
                    done[0] += 1

            norms = [0]

            def rstd(cols, width, ready=None):
                m, guess, y, p = (newt[:, k, 0:cols] for k in range(4))
                link(V.tensor_scalar(m, sums[:, 0:cols], 1.0 / width, EPS, ALU.mult, ALU.add))
                link(V.tensor_scalar(guess.bitcast(U32), m.bitcast(U32), 1, None, ALU.logical_shift_right))
                link(V.tensor_scalar(y.bitcast(I32), guess.bitcast(I32), -1.0, float(0x5F3759DF), ALU.mult, ALU.add))
                for step in range(3):
                    link(V.scalar_tensor_tensor(p, y, -0.5, m, ALU.mult, ALU.mult))
                    link(V.tensor_tensor(p, p, y, ALU.mult))
                    ins = V.scalar_tensor_tensor(y, p, 1.5, y, ALU.add, ALU.mult)
                    if step < 2 or ready is None:
                        link(ins)
                if ready is not None:
                    norms[0] += 1
                    ins.then_inc(ready, 1)
                    dve.wait_ge(ready, norms[0])
                return y

            def norm(j):
                dve.wait_ge(sq_done, 2 * j + 2)
                r = rstd(2, D, r_ready)
                V.tensor_scalar(xn[:, 0], x[:, 0], r[:, 0:1], None, ALU.mult).then_inc(xn_done, 1)

            def flat(a):
                return a.rearrange("p c n -> p (c n)")

            def gained(stage_name, hi, lo, gain, shift=None, npairs=4, bank_of=TBANK, ntiles=CT):
                for j in range(npairs):
                    dve.wait_ge(in_hi, PAIR0[stage_name] + j + 1)
                    for q in range(min(2, ntiles - 2 * j)):
                        c = 2 * j + q
                        src = ps[:, bank_of[j], q * S:(q + 1) * S]
                        if shift is None:
                            ins = V.scalar_tensor_tensor(lo[:, c], src, gain(c), hi[:, c].bitcast(F32),
                                                         ALU.mult, ALU.subtract)
                        else:
                            if j >= 2 and q == 0:
                                dve.wait_ge(in_ready, PAIR0[stage_name] + j - 1)
                            ins = V.tensor_scalar(tmp2[:, j % 2, q * S:(q + 1) * S], src, gain(c), shift(c),
                                                  ALU.mult, ALU.add)
                    if shift is not None:
                        link(ins)
                        ins = V.tensor_tensor(flat(lo[:, 2 * j:2 * j + 2]), tmp2[:, j % 2],
                                              flat(hi[:, 2 * j:2 * j + 2]).bitcast(F32), ALU.subtract)
                    ins.then_inc(in_ready, 1)

            def plain(stage_name, j, hi, lo):
                dve.wait_ge(in_hi, PAIR0[stage_name] + j + 1)
                V.tensor_tensor(flat(lo[:, 2 * j:2 * j + 2]), bank(TBANK[j]),
                                flat(hi[:, 2 * j:2 * j + 2]).bitcast(F32), ALU.subtract).then_inc(in_ready, 1)

            def tok_copy(idx, b0, dst):
                dve.wait_ge(w_used, TOK_END[idx])
                V.tensor_copy(dst, banks(b0 + 2, dst.shape[1])).then_inc(tok_copied2, 1)

            def head_max(hg, h, src, scale):
                b = h % 2
                V.reduce_max(mx[:, b, 0:1], src[:, 0:P], AX_X)
                link(V.reduce_max(mx[:, b, 1:2], src[:, P:SEG], AX_X))
                if h >= 2:
                    dve.wait_ge(exped, hg - 1)
                V.tensor_scalar(nmx[:, b], mx[:, b], -scale, None, ALU.mult).then_inc(maxed, 1)

            def o_half(hg, count, half):
                dve.wait_ge(exped, hg)
                hs_ = slice(half * count // 2, (half + 1) * count // 2)
                link(V.reciprocal(rinv[:, :, hs_], rs[:, :, hs_]))
                dve.wait_ge(pv_done, hg)
                w = D // count
                for t in range(TT):
                    V.tensor_tensor(xn[:, t, half * 512:half * 512 + 512].rearrange("p (h n) -> p h n", n=w),
                                    bank(4 + 2 * t + half).rearrange("p (h n) -> p h n", n=w),
                                    rinv[:, t, hs_].unsqueeze(2).to_broadcast([P, count // 2, w]),
                                    ALU.mult).then_inc(o_ready, 1)

            def block_heads(h0, biased_head, stage_name):
                scale = DH ** -0.5

                def normalise(h):
                    dve.wait_ge(exped, h0 + h + 1)
                    link(V.reciprocal(rinv[:, :, h:h + 1], rs[:, :, h:h + 1]))
                    w = pb[:, h % 2]
                    V.tensor_scalar(w[:, 0:P], w[:, 0:P], rinv[:, 0, h:h + 1], None, ALU.mult)
                    V.tensor_scalar(w[:, P:SEG], w[:, P:SEG], rinv[:, 1, h:h + 1], None,
                                    ALU.mult).then_inc(p_normed, 1)

                for h in range(H):
                    dve.wait_ge(scored, h0 + h + 1)
                    if biased_head:
                        if h >= 2:
                            dve.wait_ge(exped, h0 + h - 1)
                        slope = float(np.float32(2.0 ** (-8.0 * (h + 1) / H)))
                        V.scalar_tensor_tensor(tb[:, h % 2], dist[:], slope / scale, bank(h % 2, SEG),
                                               ALU.mult, ALU.add).then_inc(biased, 1)
                        dve.wait_ge(biased, h + 1)
                        head_max(h0 + h, h, tb[:, h % 2], scale)
                    else:
                        head_max(h0 + h, h, bank(h % 2, SEG), scale)
                    if h:
                        normalise(h - 1)
                    if h >= 7 and h % 4 == 3:
                        plain(stage_name, h // 4 - 1, ah, al)
                normalise(H - 1)
                plain(stage_name, 3, ah, al)

            def heads(h0, count, scale):
                for h in range(count):
                    dve.wait_ge(scored, h0 + h + 1)
                    head_max(h0 + h, h, bank(h % 2, SEG), scale)
                    if h == count // 2 + 2:
                        o_half(h0 + count // 2, count, 0)
                o_half(h0 + count, count, 1)

            def residual_wait(idx, t):
                if t == 0:
                    dve.wait_ge(half_done, idx + 1)
                else:
                    dve.wait_ge(w_used, RES_END[idx])

            def residual(idx):
                for t in range(TT):
                    residual_wait(idx, t)
                    V.tensor_tensor(x[:, t], x[:, t], banks(2 * t, D), ALU.add).then_inc(x_ready, 1)

            def gated_residual(idx):
                for t in range(TT):
                    residual_wait(idx, t)
                    link(V.tensor_tensor(xn[:, t], gB[:], banks(2 * t, D), ALU.mult))
                    V.tensor_tensor(x[:, t], x[:, t], xn[:, t], ALU.add).then_inc(x_ready, 1)

            def chunk(cs, b, silu, buf):
                dve.wait_ge(gated, cs + 1)
                if not isinstance(cs, int) or cs > 0:
                    dve.wait_ge(h_ready, cs)
                if silu:
                    V.tensor_tensor(hs, hr, bank(b + 1), ALU.mult).then_inc(h_sq, 1)
                else:
                    V.tensor_tensor(hs, hr, hr, ALU.mult).then_inc(h_sq, 1)
                dve.wait_ge(h_sq, cs + 1)
                dve.wait_ge(h_hi, cs + 1)
                V.tensor_tensor(flat(hl[:, buf]), hs, flat(hh[:, buf]).bitcast(F32), ALU.subtract).then_inc(h_ready, 1)

            def mlp(n0, c0):
                def body(i):
                    for j in range(MLP_BODY):
                        chunk(i * MLP_BODY + (c0 + j), 4 + j, False, j)
                        for q in range(2):
                            u = n0 + 2 * j + 2 + q
                            split(u if isinstance(i, int) else (u, i), slot(u))
                body(0)
                with dve.Fori(1, (CH1 - 1) // MLP_BODY) as i:
                    body(i)
                done[0] = n0 + N_MLP
                chunk(c0 + CH1 - 1, 4, False, 0)

            def swiglu(n0, c0):
                def body(i):
                    for j in range(FFN_BODY):
                        u = n0 + 3 * j + 2
                        split(u if isinstance(i, int) else (u, i), slot(u))
                        chunk(i * FFN_BODY + (c0 + j), 4 + 2 * j, True, j)
                        for q in (1, 2):
                            split(u + q if isinstance(i, int) else (u + q, i), slot(u + q))
                body(0)
                with dve.Fori(1, (CH2 - 1) // FFN_BODY) as i:
                    body(i)
                done[0] = n0 + N_FFN - 1
                splits(n0 + N_FFN - 1)
                chunk(c0 + CH2 - 1, 4, True, 0)

            def modulation(k, normw):
                dve.wait_ge(a_red, k + 1)
                b0 = COL_B["b_ada_2"] + ADA_TILES * k
                link(V.tensor_tensor(modT[:, k], bank(7, ADA_TILES), vB[:, b0:b0 + ADA_TILES], ALU.add))
                w0 = COL_A[normw]
                V.scalar_tensor_tensor(mgain[:, k], modT[:, k, CT:2 * CT], 1.0, vA[:, w0:w0 + CT],
                                       ALU.add, ALU.mult).then_inc(mod_done, 1)

            def gate_diag(k):
                V.tensor_tensor(diag, ident[:].unsqueeze(1).to_broadcast([P, CT, P]),
                                modT[:, k, 2 * CT:3 * CT].unsqueeze(2).to_broadcast([P, CT, P]),
                                ALU.mult).then_inc(diag_done, 1)

            def gate_copy(k, b0, factor):
                dve.wait_ge(gate_ps, k + 1)
                V.tensor_scalar(gB[:], banks(b0, D), factor, None, ALU.mult).then_inc(gate_done, 1)

            def log1p(k):
                dve.wait_ge(sp_exp, k)
                V.tensor_scalar(sm[:, 3], sm[:, 2], 1.0, None, ALU.add).then_inc(sp_one, 1)
                dve.wait_ge(sp_one, k)
                link(V.scalar_tensor_tensor(sm[:, 1], sm[:, 3], -1.0, sm[:, 2], ALU.add, ALU.subtract))
                link(V.reciprocal(sm[:, 6], sm[:, 3]))
                link(V.tensor_tensor(sm[:, 1], sm[:, 1], sm[:, 6], ALU.mult))
                dve.wait_ge(sp_ln, k)
                link(V.tensor_tensor(sm[:, 4], sm[:, 4], sm[:, 1], ALU.subtract))

            def rows_lo(k):
                dve.wait_ge(crow_hi, k)
                V.tensor_tensor(rowl[0:H], rowf[0:H], rowh[0:H].bitcast(F32), ALU.subtract).then_inc(crow_done, 1)

            def by_t(ap):
                return ap.rearrange("p (t n) -> p t n", t=TT)

            def gcol(name, off=0):
                return lambda c: vA[:, COL_A[name] + off + c:COL_A[name] + off + c + 1]

            norm(0)
            dve.wait_ge(rows_T, 1)
            V.tensor_copy(vA[:], bank(0, NA))
            V.tensor_copy(vB[:], ps[:, 0, P:P + NB]).then_inc(vecs, 1)
            dve.wait_ge(vecs, 1)
            gained("attn0", ah, al, gcol("attn_norm"))
            splits(2)
            dve.wait_ge(wf_hi, 1)
            V.tensor_tensor(wfl[:], wf[:], wfh[:].bitcast(F32), ALU.subtract).then_inc(wf_done, 1)
            for m in range(8):
                splits(m + 3)
            splits(U_WO0 + 1)
            tok_copy(0, 0, vt[:, 1])
            splits(U_WO0 + 2)
            dve.wait_ge(const, 1)
            block_heads(0, True, "o0")
            splits(U_MLP0 + 1)
            residual(0)
            norm(1)
            modulation(0, "norm_ffn1_2")
            gained("mlp0", ah, al, gcol("mlp_norm"))
            mlp(U_MLP0, 0)
            splits(U_K + 1)
            residual(1)
            norm(2)
            modulation(1, "norm_mix_2")
            gained("kv", ah, al, gcol("kv_norm"))
            gained("q", bh, bl, gcol("attn_norm", CT))
            splits(U_K + 2)
            dve.wait_ge(f_ps, 1)
            V.tensor_copy(rowf[0:H], ps[0:H, 3, 0:S]).then_inc(f_copied, 1)
            dve.wait_ge(f_done, 1)
            link(V.tensor_tensor(by_t(sm[:, 0]), by_t(bank(3, TT * H)), hb[:, 0:1].to_broadcast([P, TT, H]), ALU.add))
            V.scalar_tensor_tensor(sm[:, 1], sm[:, 0], -1.0, sm[:, 0], ALU.mult, ALU.min).then_inc(sp_in, 1)
            log1p(1)
            V.scalar_tensor_tensor(sm[:, 5], sm[:, 0], 0.0, sm[:, 4], ALU.min, ALU.subtract).then_inc(lf_done, 1)
            splits(U_K + 6)
            dve.wait_ge(crow_ps, 1)
            V.tensor_scalar(rowf[0:H], ps[0:H, 3, 0:S], -(DH ** 0.5), None, ALU.mult).then_inc(row_f, 1)
            rows_lo(1)
            splits(U_Q + 1)
            tok_copy(1, 4, vt[:, 1])
            splits(U_WO1 + 2)
            block_heads(H, False, "o1")
            splits(U_MLP1 + 1)
            residual(2)
            norm(3)
            modulation(2, "norm_ffn2_2")
            gained("mlp1", ah, al, gcol("mlp_norm", CT))
            mlp(U_MLP1, CHUNK0["mlp1"])
            gate_diag(0)
            splits(U_FFN1 + 1)
            residual(3)
            dve.wait_ge(sq_done, 2 * 4 + 2)
            dve.wait_ge(nb_landed, 16)
            r = rstd(2, D)
            for t in range(TT):
                V.scalar_tensor_tensor(x[:, t], x[:, t], r[:, t:t + 1], nB[:], ALU.mult, ALU.mult).then_inc(x_ready, 1)
            norm(5)

            def mod(k):
                return lambda c: mgain[:, k, c:c + 1], lambda c: modT[:, k, c:c + 1]

            gained("ffn1", ah, al, *mod(0))
            swiglu(U_FFN1, CHUNK0["ffn1"])
            splits(U_TAIL + 1)
            dve.wait_ge(gate_done, 1)
            gated_residual(4)
            norm(6)
            gained("mix", ah, al, *mod(1))

            ang, turns, red = (trig[:, k].rearrange("p (k t j) -> p k t j", k=2, t=TT) for k in range(3))
            dve.wait_ge(small_landed, 16 * (5 + TT))
            for j in range(16):
                ins = V.memset(trig[:, 3, j:j + 1], float(np.float32(10000.0 ** (-2.0 * j / ROPE))))
            link(ins)
            link(V.tensor_copy(newt[:, 4, 0:TT], posi[:]))
            for t in range(TT):
                for k in range(2):
                    ins = V.tensor_scalar(ang[:, k, t], trig[:, 3, 0:16], newt[:, 4, t:t + 1], None, ALU.mult)
            link(ins)
            two_pi, rnd = 2 * np.pi, 12582912.0
            link(V.tensor_scalar(turns[:, 0], ang[:, 0], float(1 / two_pi), rnd, ALU.mult, ALU.add))
            link(V.tensor_scalar(turns[:, 1], ang[:, 1], float(1 / two_pi), 0.25, ALU.mult, ALU.add))
            link(V.tensor_scalar(turns[:, 1], turns[:, 1], rnd, None, ALU.add))
            link(V.tensor_scalar(trig[:, 1], trig[:, 1], -rnd, None, ALU.add))
            c1 = 6.28125
            c2 = float(np.float32(two_pi - c1))
            link(V.scalar_tensor_tensor(trig[:, 2], trig[:, 1], -c1, trig[:, 0], ALU.mult, ALU.add))
            link(V.tensor_scalar(red[:, 1], red[:, 1], float(np.pi / 2), None, ALU.add))
            link(V.scalar_tensor_tensor(trig[:, 2], trig[:, 1], -c2, trig[:, 2], ALU.mult, ALU.add))
            V.tensor_scalar(trig[:, 2], trig[:, 2], 3.1415925, -3.1415925, ALU.min, ALU.max).then_inc(ang_done, 1)
            splits(U_TAIL + 5)

            dve.wait_ge(w_used, TOK_END[2])
            V.tensor_copy(tail[:, 1], banks(2, TAILW)).then_inc(tail_dve, 1)
            dve.wait_ge(tail_dve, 1)
            dve.wait_ge(tail_act, 1)
            link(V.tensor_tensor(by_t(sm[:, 0]), tail[:, :, DT0:DT0 + H], hb[:, 1:2].to_broadcast([P, TT, H]), ALU.add))
            V.scalar_tensor_tensor(sm[:, 1], sm[:, 0], -1.0, sm[:, 0], ALU.mult, ALU.min).then_inc(sp_in, 1)
            dve.wait_ge(lat_sq, 1)
            link(V.tensor_scalar(sums[:, 0:2], sums[:, 0:2], KVL / QL, None, ALU.mult))
            r = rstd(4, KVL)
            for t in range(TT):
                V.tensor_scalar(xn[:, t, 0:QL], tail[:, t, CQ0:CQ0 + QL], r[:, t:t + 1], None, ALU.mult)
                ins = V.tensor_scalar(xn[:, t, QL:QL + KVL], tail[:, t, CKV0:CKV0 + KVL], r[:, 2 + t:3 + t],
                                      None, ALU.mult)
            ins.then_inc(lat_done, 1)
            log1p(2)
            link(V.scalar_tensor_tensor(sm[:, 5], sm[:, 0], 0.0, sm[:, 4], ALU.max, ALU.add))
            dve.wait_ge(al_exp, 1)
            V.scalar_tensor_tensor(by_t(sm[:, 6]), by_t(sm[:, 5]), -1.0,
                                   aexp[:].unsqueeze(1).to_broadcast([P, TT, H]), ALU.mult, ALU.mult).then_inc(ssd_in, 1)
            dve.wait_ge(trig_done, 1)
            sc = trig[:, 3].rearrange("p (k t j) -> p k t j", k=2, t=TT)
            kt4 = ktok.rearrange("p t (h n) -> p t h n", h=HM)
            u1, u2 = tail[:, :, KR0:KR0 + 16], tail[:, :, KR0 + 16:KR0 + 32]
            r4 = [rope[:, k, 0:32].rearrange("p (t j) -> p t j", t=TT) for k in range(4)]
            for k, (u, w) in enumerate(((u1, 1), (u2, 0), (u2, 1), (u1, 0))):
                ins = V.tensor_tensor(r4[k], u, sc[:, w], ALU.mult)
            link(ins)
            for t in range(TT):
                wide = [a[:, t:t + 1].to_broadcast([P, HM, 16]) for a in r4]
                V.tensor_tensor(kt4[:, t, :, NOPE:NOPE + 16], wide[0], wide[1], ALU.subtract)
                V.tensor_tensor(kt4[:, t, :, NOPE + 16:QK], wide[2], wide[3], ALU.add)
            splits(U_Z + 5)
            gained("lat", bh, bl, gcol("q_norm_w_2"), npairs=3, bank_of=[0, 1, 2], ntiles=5)
            splits(U_UKV + 1)
            dve.wait_ge(w_used, U_UKV)
            V.tensor_copy(qtok[:, 1], banks(6, 768)).then_inc(mq_tok2, 1)
            for half in range(2):
                dve.wait_ge(w_used, U_UKV + 1 + half)
                src = banks(4 * half + 2, 768).rearrange("p (h n) -> p h n", h=4)
                V.tensor_copy(kt4[:, 1, 4 * half:4 * half + 4, 0:NOPE], src[:, :, 0:NOPE])
                V.tensor_copy(vm[:, 1].rearrange("p (h n) -> p h n", h=HM)[:, 4 * half:4 * half + 4],
                              src[:, :, NOPE:192]).then_inc(mq_tok2, 1)
            dve.wait_ge(mq_tok, 1)
            dve.wait_ge(mq_tok2, 1)
            qt4 = qtok.rearrange("p t (h n) -> p t h n", h=HM)
            for t in range(TT):
                q1, q2 = qt4[:, t, :, NOPE:NOPE + 16], qt4[:, t, :, NOPE + 16:QK]
                w4 = [rope[:, k, P * t:P * t + P].rearrange("p (h j) -> p h j", h=HM) for k in range(4)]
                for k, (u, w) in enumerate(((q1, 1), (q2, 0), (q2, 1), (q1, 0))):
                    ins = V.tensor_tensor(w4[k], u, sc[:, w, t:t + 1].to_broadcast([P, HM, 16]), ALU.mult)
                link(ins)
                V.tensor_tensor(q1, w4[0], w4[1], ALU.subtract)
                ins = V.tensor_tensor(q2, w4[2], w4[3], ALU.add)
            ins.then_inc(qtok_done, 1)
            splits(U_XBC + 1)
            for u in range(6):
                dve.wait_ge(conv0, u + 1)
                for k in range(1, 4):
                    for q in range(2):
                        acc = conv_buf(u)[:, q, k:S]
                        ins = V.scalar_tensor_tensor(acc, ps[:, u % 3, q * S:(q + 1) * S - k], conv_w(3 - k, 2 * u + q),
                                                     acc, ALU.mult, ALU.add)
                    if k < 3:
                        link(ins)
                ins.then_inc(conv_acc, 1)
                splits(U_XBC + u + 2)
            splits(U_OUT + 2)
            dve.wait_ge(xs_T, 1)
            V.tensor_copy(xs[:, 1], banks(6, D)).then_inc(xs_tok2, 1)
            dve.wait_ge(xs_tok, 1)
            dve.wait_ge(xs_tok2, 1)

            def by_head(a):
                return a.rearrange("p (h n) -> p h n", h=H)

            for t in range(TT):
                ins = V.tensor_tensor(by_head(xdt[:, t]), by_head(xs[:, t]),
                                      by_t(sm[:, 5])[:, t].unsqueeze(2).to_broadcast([P, H, DH]), ALU.mult)
            ins.then_inc(xdt_done, 1)
            dve.wait_ge(xdt_done, 1)
            for t in range(TT):
                V.tensor_tensor(by_head(xs[:, t]), by_head(xs[:, t]),
                                hb[:, 3].unsqueeze(2).to_broadcast([P, H, DH]), ALU.mult)
            dve.wait_ge(mqk_T, 1)
            for b in range(4):
                ins = V.tensor_copy(kTm[b // 2][0:QK, 2 * (b % 2):2 * (b % 2) + 2],
                                    ps[0:QK, b].rearrange("p (h n) -> p h n", h=2))
            ins.then_inc(mqk_copied2, 1)
            heads(2 * H, HM, QK ** -0.5)
            dve.wait_ge(mla_sq, 1)
            r = rstd(2, D)
            for t in range(TT):
                V.tensor_scalar(xn[:, t], xn[:, t], r[:, t:t + 1], None, ALU.mult).then_inc(mla_done, 1)
            gained("mla", bh, bl, gcol("mla_norm_w_2"))
            dve.wait_ge(cb_ps, 1)
            for gr in range(2):
                V.tensor_copy(cb[:, gr], bank(gr, SEG))
            V.tensor_scalar(sm[:, 7], bank(2, TT * H), -1.0, None, ALU.mult).then_inc(ac_done, 1)
            V.tensor_copy(rowf[0:H], ps[0:H, 3, 0:S]).then_inc(row_f, 1)
            gate_diag(1)
            rows_lo(2)
            gate_copy(1, 2, 1.0)
            for h in range(H):
                dve.wait_ge(dec_exp, h + 1)
                if h >= 2:
                    dve.wait_ge(y_done, h - 1)
                V.tensor_tensor(pb[:, h % 2], tb[:, h % 2], cb[:, h // CT], ALU.mult).then_inc(dec_m, 1)
            dve.wait_ge(y_done, H)
            dve.wait_ge(z_done, 1)
            for t in range(TT):
                link(V.tensor_tensor(xs[:, t], xs[:, t], banks(4 + 2 * t, D), ALU.add))
                V.tensor_tensor(xs[:, t], xs[:, t], z[:, t], ALU.mult).then_inc(y_ready, 1)
            dve.wait_ge(ssd_sq, 2)
            r = rstd(4, 512)
            for t in range(TT):
                for gr in range(2):
                    half = xs[:, t, 512 * gr:512 * gr + 512]
                    ins = V.tensor_scalar(half, half, r[:, 2 * t + gr:2 * t + gr + 1], None, ALU.mult)
                ins.then_inc(y_ready, 1)
            splits(U_OUT + 3)
            gained("ssd", ah, al, gcol("ssd_norm_w_2"))
            gate_diag(2)
            splits(U_FFN2 + 1)
            gated_residual(5)
            norm(7)
            gained("ffn2", ah, al, *mod(2))
            swiglu(U_FFN2, CHUNK0["ffn2"])
            dve.wait_ge(gate_done, 3)
            gated_residual(6)
            dve.wait_ge(sq_done, 2 * 8 + 2)
            dve.wait_ge(nb_landed, 32)
            r = rstd(2, D)
            for t in range(TT):
                V.scalar_tensor_tensor(x[:, t], x[:, t], r[:, t:t + 1], nB[:], ALU.mult, ALU.mult).then_inc(out_ready, 1)

        @block.tensor
        def _(pe):
            T = nc.tensor

            def unit_wait(n):
                if isinstance(n, int):
                    pe.wait_ge(w_lo, n + 1)
                else:
                    pe.wait_ge(w_lo, n[1] * 6 + (n[0] + 1))

            def a_unit(n, s, b, xh, xl, stage_name=None):
                unit_wait(n)
                wh, wl = w_view(whi, s, CT, AW), w_view(wlo, s, CT, AW)
                for m in range(AW // P):
                    o = ps[:, b, m * S:(m + 1) * S]
                    for c in range(CT):
                        if stage_name and m == 0 and c % 2 == 0:
                            pe.wait_ge(in_ready, PAIR0[stage_name] + c // 2 + 1)
                        wmh, wml = wh[:, c, m * P:(m + 1) * P], wl[:, c, m * P:(m + 1) * P]
                        T.matmul(o, wmh, xh[:, c], start=(c == 0), stop=False)
                        T.matmul(o, wmh, xl[:, c], start=False, stop=False)
                        ins = T.matmul(o, wml, xh[:, c], start=False, stop=(c == CT - 1))
                ins.then_inc(w_used, 1)

            def last_d_unit(n, s, xh, xl, c0):
                unit_wait(n)
                wh, wl = w_view(whi, s, 2, D), w_view(wlo, s, 2, D)
                for t in range(TT):
                    tt = slice(t * P, (t + 1) * P)
                    for k in range(2):
                        for a_, w_, end in ((xh, wh, False), (xh, wl, False), (xl, wh, k == 1)):
                            for v in range(2):
                                ins = T.matmul(ps[:, 2 * t + v], a_[:, c0 + k, tt], w_[:, k, v * 512:v * 512 + 512],
                                               start=False, stop=end)
                    ins.then_inc(half_done if t == 0 else w_used, 1)

            def d_unit(n, s, b0, kn, width, xh, xl, c0, first, last, stage_name=None):
                unit_wait(n)
                wh, wl = w_view(whi, s, kn, width), w_view(wlo, s, kn, width)
                for k in range(kn):
                    c = c0 + k
                    if stage_name and c % 2 == 0:
                        pe.wait_ge(in_ready, PAIR0[stage_name] + c // 2 + 1)
                    for t in range(TT):
                        tt = slice(t * P, (t + 1) * P)
                        outs = [(ps[:, b0 + 2 * t + v // 512, 0:min(512, width - v)], v, min(v + 512, width))
                                for v in range(0, width, 512)]
                        for o, v, e in outs:
                            T.matmul(o, xh[:, c, tt], wh[:, k, v:e], start=(first and k == 0), stop=False)
                        for o, v, e in outs:
                            T.matmul(o, xh[:, c, tt], wl[:, k, v:e], start=False, stop=False)
                        for o, v, e in outs:
                            ins = T.matmul(o, xl[:, c, tt], wh[:, k, v:e], start=False, stop=(last and k == kn - 1))
                ins.then_inc(w_used, 1)

            def d_units(n0, count, b0, xh, xl, stage_name=None, width=D, start=True):
                for u in range(count):
                    d_unit(n0 + u, slot(n0 + u), b0, 2, width, xh, xl, 2 * u, start and u == 0, u == count - 1,
                           stage_name)

            def transposes(src, ready, bank_of=TBANK, ntiles=CT, before=None):
                for t in range(TT):
                    pe.wait_ge(*ready[t])
                    for c in range(ntiles):
                        if t == 0 and before and c in before:
                            pe.wait_ge(*before[c])
                        o = ps[:, bank_of[c // 2], (c % 2) * S + t * P:(c % 2) * S + (t + 1) * P]
                        ins = T.transpose(o, src[:, t, c * P:(c + 1) * P], ident[:])
                        if t == TT - 1 and (c % 2 == 1 or c == ntiles - 1):
                            ins.then_inc(tr_done, 1)

            def norm_T(j, before=None):
                n = (j if j < 4 else j - 1) + 1
                transposes(xn, [(xn_done, n), (xn1_done, n)], before=before)

            def heads(h0, count, score, vals, w):
                def weights_T(h):
                    pe.wait_ge(exped, h0 + h + 1)
                    if h >= 2:
                        pe.wait_ge(p_copied, h0 + h - 1)
                    for k in range(3):
                        ins = T.transpose(ps[:, 2 + h % 2, k * P:(k + 1) * P], pb[:, h % 2, k * P:(k + 1) * P], ident[:])
                    ins.then_inc(p_tr, 1)

                def values(h):
                    pe.wait_ge(p_copied, h0 + h + 1)
                    half, hc = divmod(h, count // 2)
                    cols = slice(hc * w, (hc + 1) * w)
                    pth = pt[:, h % 2]
                    v = [vals[:, t, h * w:(h + 1) * w] for t in range(TT)]
                    T.matmul(ps[:, 4 + half, cols], pth[:, 0:P], v[0], start=True, stop=True)
                    T.matmul(ps[:, 6 + half, cols], pth[:, P:S], v[0], start=True, stop=False)
                    T.matmul(ps[:, 6 + half, cols], pth[:, S:SEG], v[1], start=False, stop=True).then_inc(pv_done, 1)

                for h in range(2):
                    score(h).then_inc(scored, 1)
                for h in range(count):
                    weights_T(h)
                    if h + 2 < count:
                        score(h + 2).then_inc(scored, 1)
                    if h:
                        values(h - 1)
                values(count - 1)

            def block_heads(h0, score, bank_free):
                def weights_T(h):
                    pe.wait_ge(p_normed, h0 + h + 1)
                    if h >= 2:
                        pe.wait_ge(p_copied, h0 + h - 1)
                    for k in range(3):
                        ins = T.transpose(ps[:, 2 + h % 2, k * P:(k + 1) * P], pb[:, h % 2, k * P:(k + 1) * P], ident[:])
                    ins.then_inc(p_tr, 1)

                def values(h):
                    pe.wait_ge(p_copied, h0 + h + 1)
                    c, r = h // 2, slice(DH * (h % 2), DH * (h % 2) + DH)
                    o = ps[r, TBANK[c // 2], (c % 2) * S:(c % 2) * S + S]
                    pth, v = pt[:, h % 2], [vt[:, t, h * DH:(h + 1) * DH] for t in range(TT)]
                    T.matmul(o, v[0], pth[:, 0:S], start=True, stop=False)
                    T.matmul(o[:, P:S], v[1], pth[:, S:SEG], start=False, stop=True).then_inc(pv_done, 1)

                for h in range(2):
                    score(h).then_inc(scored, 1)
                for h in range(H):
                    if h + 2 < H:
                        pe.wait_ge(bank_free, h0 + h + 1)
                        score(h + 2).then_inc(scored, 1)
                    weights_T(h)
                    if h:
                        values(h - 1)
                values(H - 1)

            def pair_score(h, rows):
                c, r = h // 2, slice(64 * (h % 2), 64 * (h % 2) + 64)
                o = bank(h % 2, SEG)
                ins = T.matmul(o[:, 0:P], qT[r, c, 0:P], kT[r, c, 0:P], start=True, stop=not rows)
                if rows:
                    mask_and_row(o, 0, h)
                ins = T.matmul(o[:, P:SEG], qT[r, c, P:S], kT[r, c, :], start=True, stop=not rows)
                return mask_and_row(o, 1, h) if rows else ins

            def mask_and_row(o, t, h):
                lo, hi = (0, P) if t == 0 else (P, SEG)
                sel = identr[:, h:h + 1].to_broadcast([P, P])
                T.matmul(o[:, hi - P:hi], identr[:], maskq[:], start=False, stop=False)
                T.matmul(o[:, lo:hi], sel, rowh[:, 0:hi - lo], start=False, stop=False)
                return T.matmul(o[:, lo:hi], sel, rowl[:, 0:hi - lo], start=False, stop=True)

            def mla_score(h):
                o = bank(h % 2, SEG)
                k = kTm[h // 4][0:QK, h % 4]
                T.matmul(o[:, 0:P], qTm[0:QK, h, 0:P], k[:, 0:P], start=True, stop=False)
                T.matmul(o[:, 0:P], identr[:], maskq[:], start=False, stop=True)
                T.matmul(o[:, P:SEG], qTm[0:QK, h, P:S], k, start=True, stop=False)
                return T.matmul(o[:, S:SEG], identr[:], maskq[:], start=False, stop=True)

            def ada_sum(k):
                pe.wait_ge(a_sum, 4 * ADA_TILES * (k + 1))
                for j in range(ADA_TILES):
                    ins = T.matmul(ps[:, 7, j:j + 1], aacc[:, j, :], cum[:, P:P + 1], start=True, stop=True)
                ins.then_inc(a_red, 1)

            def gate_rows(k, b):
                pe.wait_ge(diag_done, k + 1)
                for q in range(2):
                    ins = T.matmul(bank(b[q]), cum[:, P:S],
                                   diag[:, 4 * q:4 * q + 4].rearrange("p c n -> p (c n)"), start=True, stop=True)
                ins.then_inc(gate_ps, 1)

            def wo_units(n0, stage_name):
                for u in range(3):
                    d_unit(n0 + u, slot(n0 + u), 0, 2, D, ah, al, 2 * u, u == 0, False, stage_name)
                pe.wait_ge(in_ready, PAIR0[stage_name] + 4)
                last_d_unit(n0 + 3, slot(n0 + 3), ah, al, 6)

            def mlp(n0, c0, stage_name):
                def up_(n, s, cs, b, name=None):
                    if not isinstance(cs, int) or cs - c0 >= MLP_BODY:
                        pe.wait_ge(gated, cs - (MLP_BODY - 1))
                    a_unit(n, s, b, ah, al, name)

                def body(i):
                    st_ = isinstance(i, int)
                    for j in range(MLP_BODY):
                        u = n0 + 1 + 2 * j
                        up_(u if st_ else (u, i), slot(u), i * MLP_BODY + (c0 + j + 1), 4 + (j + 1) % MLP_BODY)
                        pe.wait_ge(h_ready, i * MLP_BODY + (c0 + j + 1))
                        d_unit(u + 1 if st_ else (u + 1, i), slot(u + 1), 0, 2, D, hh[:, j], hl[:, j], 0,
                               st_ and j == 0, False)

                up_(n0, slot(n0), c0, 4, stage_name)
                body(0)
                with pe.Fori(1, (CH1 - 1) // MLP_BODY) as i:
                    body(i)
                pe.wait_ge(h_ready, c0 + CH1)
                last_d_unit(n0 + N_MLP - 1, slot(n0 + N_MLP - 1), hh[:, 0], hl[:, 0], 0)

            def swiglu(n0, c0, stage_name):
                def pair(u, i, cs, b, name=None):
                    if not isinstance(cs, int) or cs - c0 >= FFN_BODY:
                        pe.wait_ge(h_sq, cs - (FFN_BODY - 1))
                    a_unit(u if i is None else (u, i), slot(u), b, ah, al, name)
                    a_unit(u + 1 if i is None else (u + 1, i), slot(u + 1), b + 1, ah, al)

                def body(i):
                    st_ = isinstance(i, int)
                    for j in range(FFN_BODY):
                        u = n0 + 2 + 3 * j
                        pair(u, None if st_ else i, i * FFN_BODY + (c0 + j + 1), 4 + 2 * ((j + 1) % FFN_BODY))
                        pe.wait_ge(h_ready, i * FFN_BODY + (c0 + j + 1))
                        d_unit(u + 2 if st_ else (u + 2, i), slot(u + 2), 0, 2, D, hh[:, j], hl[:, j], 0,
                               st_ and j == 0, False)

                pair(n0, None, c0, 4, stage_name)
                body(0)
                with pe.Fori(1, (CH2 - 1) // FFN_BODY) as i:
                    body(i)
                pe.wait_ge(h_ready, c0 + CH2)
                last_d_unit(n0 + N_FFN - 1, slot(n0 + N_FFN - 1), hh[:, 0], hl[:, 0], 0)

            pe.wait_ge(const, 1)
            pe.wait_ge(rows_landed, 16 * (len(ROWS_A) + len(ROWS_B)))
            T.transpose(ps[:, 0, 0:NA], rows[0:NA, 0, :], ident[0:NA, 0:NA])
            T.transpose(ps[:, 0, P:P + NB], rows[0:NB, 1, :], ident[0:NB, 0:NB]).then_inc(rows_T, 1)
            norm_T(0)
            for m in range(8):
                if m >= 3:
                    pe.wait_ge(qk_copied, m - 2)
                a_unit(U_QK + m, slot(U_QK + m), qk_bank(m), ah, al, "attn0" if m == 0 else None)
            d_units(U_V, 4, 0, ah, al)
            pe.wait_ge(qk_copied, 8)
            pe.wait_ge(tok_copied, 1)
            pe.wait_ge(tok_copied2, 1)
            block_heads(0, lambda h: pair_score(h, False), biased)
            wo_units(U_WO0, "o0")
            ada_sum(0)
            norm_T(1, {6: (mod_done, 1)})
            mlp(U_MLP0, 0, "mlp0")

            ada_sum(1)
            norm_T(2, {6: (mod_done, 2)})
            pe.wait_ge(wf_done, 1)
            for c in range(CT):
                if c % 2 == 0:
                    pe.wait_ge(in_ready, PAIR0["kv"] + c // 2 + 1)
                o = ps[0:H, 3, 0:S]
                T.matmul(o, wfh[:, c], ah[:, c], start=(c == 0), stop=False)
                T.matmul(o, wfh[:, c], al[:, c], start=False, stop=False)
                ins = T.matmul(o, wfl[:, c], ah[:, c], start=False, stop=(c == CT - 1))
            ins.then_inc(f_ps, 1)
            for m in range(8, 12):
                pe.wait_ge(qk_copied, m - 1)
                a_unit(U_K + m - 8, slot(U_K + m - 8), qk_bank(m), ah, al)
                if m == 8:
                    pe.wait_ge(f_copied, 1)
                    for t in range(TT):
                        ins = T.transpose(ps[:, 3, t * H:(t + 1) * H], rowf[0:H, t * P:(t + 1) * P], ident[0:H, 0:H])
                    ins.then_inc(f_done, 1)
            pe.wait_ge(lf_done, 1)
            lf = sm[:, 5].rearrange("p (t h) -> p t h", t=TT)
            T.matmul(ps[0:H, 3, 0:S], lf[:, 0], cum[:], start=True, stop=False)
            T.matmul(ps[0:H, 3, P:S], lf[:, 1], cum[:, 0:P], start=False, stop=True).then_inc(crow_ps, 1)
            pe.wait_ge(in_ready, PAIR0["q"] + 4)
            d_units(U_VS, 4, 4, ah, al)
            for m in range(12, 16):
                pe.wait_ge(qk_copied, m - 1)
                a_unit(U_Q + m - 12, slot(U_Q + m - 12), qk_bank(m), bh, bl)
            pe.wait_ge(qk_copied, 16)
            pe.wait_ge(tok_copied, 2)
            pe.wait_ge(tok_copied2, 2)
            pe.wait_ge(crow_done, 1)
            block_heads(H, lambda h: pair_score(h, True), exped)
            wo_units(U_WO1, "o1")
            ada_sum(2)
            norm_T(3, {6: (mod_done, 3)})
            mlp(U_MLP1, CHUNK0["mlp1"], "mlp1")
            gate_rows(0, (5, 7))
            norm_T(5, {4: (gate_done, 1)})
            swiglu(U_FFN1, CHUNK0["ffn1"], "ffn1")

            norm_T(6)
            d_units(U_TAIL, 4, 0, ah, al, "mix", width=TAILW)
            d_units(U_Z, 4, 4, ah, al)
            pe.wait_ge(tail_act, 1)
            pe.wait_ge(tail_dve, 1)
            transposes(xn, [(lat_done, 1)] * TT, [0, 1, 2], 5)
            pe.wait_ge(z_done, 1)
            pe.wait_ge(in_ready, PAIR0["lat"] + 3)
            d_unit(U_UQ, slot(U_UQ), 4, 2, 768, bh, bl, 0, True, False)
            d_unit(U_UQ + 1, slot(U_UQ + 1), 4, 1, 768, bh, bl, 2, False, True)
            d_unit(U_UKV, slot(U_UKV), 0, 2, 768, bh, bl, 3, True, True)
            pe.wait_ge(mq_tok, 1)
            pe.wait_ge(mq_tok2, 1)
            d_unit(U_UKV + 1, slot(U_UKV + 1), 4, 2, 768, bh, bl, 3, True, True)
            pe.wait_ge(mq_tok, 2)
            pe.wait_ge(mq_tok2, 2)
            for u in range(6):
                if u >= 3:
                    pe.wait_ge(conv_acc, u - 2)
                a_unit(U_XBC + u, slot(U_XBC + u), u % 3, ah, al)
            pe.wait_ge(mq_tok, 3)
            pe.wait_ge(mq_tok2, 3)
            pe.wait_ge(conv_out, 4)
            for t in range(TT):
                for c in range(CT):
                    ins = T.transpose(ps[:, 4 + 2 * t + c // 4, (c % 4) * P:(c % 4 + 1) * P],
                                      xsT[:, c, t * P:(t + 1) * P], ident[:])
            ins.then_inc(xs_T, 1)
            pe.wait_ge(qtok_done, 1)
            pe.wait_ge(conv_acc, 6)
            for b, src in ((0, ktok), (4, qtok)):
                if b:
                    pe.wait_ge(xs_tok, 1)
                    pe.wait_ge(xs_tok2, 1)
                for h in range(HM):
                    for t in range(TT):
                        ins = T.transpose(ps[0:QK, b + h // 2, (h % 2) * S + t * P:(h % 2) * S + (t + 1) * P],
                                          src[:, t, h * QK:(h + 1) * QK], ident[:])
            ins.then_inc(mqk_T, 1)
            pe.wait_ge(mqk_copied, 1)
            pe.wait_ge(mqk_copied2, 1)
            heads(2 * H, HM, mla_score, vm, VH)
            transposes(xn, [(mla_done, t + 1) for t in range(TT)])
            pe.wait_ge(conv_out, 6)
            pe.wait_ge(ssd_in, 1)
            for gr in range(2):
                b_g, c_g = bc[:, gr], bc[:, 2 + gr]
                T.matmul(ps[:, gr, 0:S], b_g[:, 0:P], c_g, start=True, stop=True)
                T.matmul(ps[:, gr, S:SEG], b_g[:, P:S], c_g[:, P:S], start=True, stop=True)
            a = sm[:, 6].rearrange("p (t h) -> p t h", t=TT)
            T.matmul(ps[:, 2, 0:H], cum[:, 0:P], a[:, 0], start=True, stop=True)
            T.matmul(ps[:, 2, H:2 * H], cum[:, P:S], a[:, 0], start=True, stop=False)
            T.matmul(ps[:, 2, H:2 * H], cum[:, 0:P], a[:, 1], start=False, stop=True)
            T.matmul(ps[0:H, 3, 0:S], a[:, 0], cum[:], start=True, stop=False)
            T.matmul(ps[0:H, 3, P:S], a[:, 1], cum[:, 0:P], start=False, stop=True).then_inc(cb_ps, 1)
            pe.wait_ge(crow_done, 2)
            gate_rows(1, (2, 3))
            pe.wait_ge(in_ready, PAIR0["mla"] + 4)
            pe.wait_ge(xdt_done, 1)

            def decay_rows(h):
                if h >= 2:
                    pe.wait_ge(dec_exp, h - 1)
                o = bank(h % 2, SEG)
                sel = identr[:, h:h + 1].to_broadcast([P, P])
                T.matmul(o[:, 0:S], sel, rowh[:], start=True, stop=False)
                T.matmul(o[:, 0:S], sel, rowl[:], start=False, stop=False)
                T.matmul(o[:, 0:P], identr[:], maskt[:], start=False, stop=True)
                T.matmul(o[:, S:SEG], sel, rowh[:, P:S], start=True, stop=False)
                T.matmul(o[:, S:SEG], sel, rowl[:, P:S], start=False, stop=False)
                T.matmul(o[:, S:SEG], identr[:], maskt[:], start=False, stop=True).then_inc(row_ps, 1)

            for h in range(2):
                decay_rows(h)
            for h in range(H):
                pe.wait_ge(dec_m, h + 1)
                if h + 2 < H:
                    decay_rows(h + 2)
                half, hc = divmod(h, 8)
                cols = slice(hc * DH, (hc + 1) * DH)
                m_, v = pb[:, h % 2], [xdt[:, t, h * DH:(h + 1) * DH] for t in range(TT)]
                T.matmul(ps[:, 4 + half, cols], m_[:, 0:P], v[0], start=True, stop=True)
                T.matmul(ps[:, 6 + half, cols], m_[:, P:S], v[0], start=True, stop=False)
                T.matmul(ps[:, 6 + half, cols], m_[:, S:SEG], v[1], start=False, stop=True).then_inc(y_done, 1)
            pe.wait_ge(gate_done, 2)
            for u in range(3):
                d_unit(U_OUT + u, slot(U_OUT + u), 0, 2, D, bh, bl, 2 * u, u == 0, False)
            transposes(xs, [(y_ready, TT + t + 1) for t in range(TT)])
            d_unit(U_OUT + 3, slot(U_OUT + 3), 0, 2, D, bh, bl, 6, False, False)
            for u in range(4, 7):
                d_unit(U_OUT + u, slot(U_OUT + u), 0, 2, D, ah, al, 2 * u - 8, False, False, "ssd")
            pe.wait_ge(in_ready, PAIR0["ssd"] + 4)
            last_d_unit(U_OUT + 7, slot(U_OUT + 7), ah, al, 6)
            gate_rows(2, (5, 7))
            norm_T(7, {4: (gate_done, 3)})
            swiglu(U_FFN2, CHUNK0["ffn2"], "ffn2")


_INS = ["x", "attn_norm", "moba_w_qkv", "fox_w_q", "w_o", "kv_norm", "w_kv", "w_f", "b_f", "mlp_norm", "w_up",
        "w_down", "final_norm", "c_2", "positions_2", "w_ada_2", "b_ada_2", "norm_ffn1_2", "ffn1_w_gate_2",
        "ffn1_w_up_2", "ffn1_w_down_2", "norm_mix_2", "w_in_2", "conv_w_2", "conv_b_2", "dt_bias_2", "a_log_2",
        "d_skip_2", "ssd_norm_w_2", "q_norm_w_2", "w_uq_2", "kv_norm_w_2", "w_ukv_2", "mla_norm_w_2", "w_out_2",
        "norm_ffn2_2", "ffn2_w_gate_2", "ffn2_w_up_2", "ffn2_w_down_2", "norm_final_2"]
_OUTS = [((1, S, D), "float32")]


def kernel(**inputs):
    import numpy as _np
    import concourse.bacc as _bacc
    from concourse import mybir as _mybir
    from concourse.bass_utils import run_bass_kernel_spmd as _run

    nc = _bacc.Bacc("TRN2", target_bir_lowering=False, num_devices=1)
    arrays, args = {}, {}
    for name in _INS:
        a = _np.ascontiguousarray(inputs[name])
        arrays[f"in_{name}_dram"] = a
        args[name] = nc.dram_tensor(f"in_{name}_dram", a.shape, _mybir.dt.from_np(a.dtype), kind="ExternalInput").ap()
    shape, dtype = _OUTS[0]
    out = nc.dram_tensor("out_0_dram", shape, _mybir.dt.from_np(_np.dtype(dtype)), kind="ExternalOutput").ap()
    build(nc, args, out)
    r = _run(nc, [arrays], core_ids=[0])
    return r.results[0]["out_0_dram"]
```
